# Optimizing a Trainium2 kernel written in Bass

```python
import jax, jax.numpy as jnp
from jax import lax
import numpy as np

D_MODEL = 1024
BATCH = 1
SEQ = 512
DEPTH = 2
DEC_BATCH = 8
DEC_SEQ = 1
PAST_LEN = 256
PAGE_SIZE = 128

HEAD_DIM = 64
N_HEADS_A = D_MODEL // HEAD_DIM
N_HEADS_B = D_MODEL // HEAD_DIM
N_KV_B = N_HEADS_B // 4
DILATED = ((128, 1), (512, 4), (2048, 16))
N_DIL = len(DILATED)
BLOCK = 128
ROT_DIM = HEAD_DIM // 4
ROPE_THETA = 500000.0
N_GROUPS = 4
EXPERTS_PER_GROUP = 8
N_EXPERTS = N_GROUPS * EXPERTS_PER_GROUP
TOP_K = 2
D_EXPERT = D_MODEL // 4
N_A_LAYERS = DEPTH // 2
N_B_LAYERS = DEPTH - N_A_LAYERS
SB_BIAS_MIN = 2.0
SB_BIAS_MAX = 8.0
RMS_EPS = 1e-6
NEG_INF = -1e30

kernel_name = "yoco_stickbreak_dilated_hmoe_step"

def rmsnorm(x, g):
    xf = x.astype(jnp.float32)
    y = xf * lax.rsqrt(jnp.mean(xf * xf, axis=-1, keepdims=True) + RMS_EPS)
    return (y * g.astype(jnp.float32)).astype(x.dtype)

def rope(x, pos):
    half = ROT_DIM // 2
    inv = jnp.power(ROPE_THETA, -jnp.arange(half, dtype=jnp.float32) * 2.0 / ROT_DIM)
    ang = pos.astype(jnp.float32)[:, None] * inv[None, :]
    cos = jnp.cos(ang)[:, None, :].astype(x.dtype)
    sin = jnp.sin(ang)[:, None, :].astype(x.dtype)
    x1, x2 = x[..., :half], x[..., half:ROT_DIM]
    return jnp.concatenate([x1 * cos - x2 * sin, x2 * cos + x1 * sin, x[..., ROT_DIM:]], axis=-1)

def sb_attend(q, k, v, q_pos, k_pos, bias):
    z = jnp.einsum('bqhe,bkhe->bhqk', q, k).astype(jnp.float32) * (HEAD_DIM ** -0.5)
    z = z + bias.astype(jnp.float32)[None, :, None, None]
    mask = k_pos[None, :] < q_pos[:, None]
    log_beta = jax.nn.log_sigmoid(z)
    log_rest = jnp.where(mask, jax.nn.log_sigmoid(-z), 0.0)
    tail = lax.cumsum(log_rest, axis=3, reverse=True) - log_rest
    a = jnp.where(mask, jnp.exp(log_beta + tail), 0.0)
    return jnp.einsum('bhqk,bkhe->bqhe', a.astype(v.dtype), v)

def sb_prompt(q, k, v, bias):
    b, s, h, e = q.shape
    nb = s // BLOCK
    qb = q.reshape(b, nb, BLOCK, h, e).swapaxes(0, 1)
    k_pos = jnp.arange(s)

    def one(args):
        q_blk, start = args
        return sb_attend(q_blk, k, v, start + jnp.arange(BLOCK), k_pos, bias)

    o = lax.map(one, (qb, jnp.arange(nb) * BLOCK))
    return o.swapaxes(0, 1).reshape(b, s, h, e)

def local_attend(q, k, v, mask):
    *lead, nq, h, e = q.shape
    hkv = k.shape[-2]
    qg = q.reshape(*lead, nq, hkv, h // hkv, e)
    s = jnp.einsum('...qhge,...che->...hgqc', qg, k).astype(jnp.float32) * (HEAD_DIM ** -0.5)
    s = jnp.where(mask[..., None, None, :, :], s, NEG_INF)
    lse = jax.nn.logsumexp(s, axis=-1)
    p = jnp.exp(s - lse[..., None])
    o = jnp.einsum('...hgqc,...che->...qhge', p.astype(v.dtype), v)
    return o.reshape(*lead, nq, h, e), jnp.moveaxis(lse, -1, -3).reshape(*lead, nq, h)

def split_residues(x, dil, n_blk):
    b, s = x.shape[:2]
    rest = x.shape[2:]
    n_sub = s // dil
    x = x.reshape(b, n_sub, dil, *rest).swapaxes(1, 2)
    x = jnp.pad(x, [(0, 0), (0, 0), (0, n_blk * BLOCK - n_sub)] + [(0, 0)] * len(rest))
    return x.reshape(b, dil, n_blk, BLOCK, *rest)

def merge_residues(x, s):
    b, dil, n_blk = x.shape[:3]
    rest = x.shape[4:]
    x = x.reshape(b, dil, n_blk * BLOCK, *rest)[:, :, : s // dil]
    return x.swapaxes(1, 2).reshape(b, s, *rest)

def band(x):
    xp = jnp.concatenate([jnp.zeros_like(x[:, :, :1]), x], axis=2)
    return jnp.concatenate([xp[:, :, :-1], xp[:, :, 1:]], axis=3)

def dilated_prompt(q, k, v, window, dil):
    s = q.shape[1]
    steps = window // dil
    nb = -(-(s // dil) // BLOCK)
    qb, kb, vb = (split_residues(t, dil, nb) for t in (q, k, v))
    blk = jnp.arange(nb)[:, None, None]
    iq = blk * BLOCK + jnp.arange(BLOCK)[None, :, None]
    ik = (blk - 1) * BLOCK + jnp.arange(2 * BLOCK)[None, None, :]
    rel = iq - ik
    mask = (rel >= 0) & (rel <= steps) & (ik >= 0)
    o, lse = local_attend(qb, band(kb), band(vb), mask)
    return merge_residues(o, s), merge_residues(lse, s)

def dilated_sample(q, buf, kv_new, window, dil):
    comb = jnp.concatenate([buf, kv_new], axis=1)
    lb, t = buf.shape[1], q.shape[1]
    steps = window // dil
    idx = lb + jnp.arange(t)[:, None] - jnp.arange(steps + 1)[None, :] * dil
    valid = idx >= 0
    sel = jnp.take(comb, jnp.maximum(idx, 0), axis=1)
    o, lse = local_attend(q[:, :, None], sel[:, :, :, 0], sel[:, :, :, 1], valid[:, None, :])
    return o[:, :, 0], lse[:, :, 0]

def combine_groups(outs, lses):
    w = jax.nn.softmax(jnp.stack(lses), axis=0).astype(outs[0].dtype)
    return jnp.einsum('gbth,gbthe->bthe', w, jnp.stack(outs))

def shared_kv(x, g_kv, w_kv, k_norm, pos):
    b, t, _ = x.shape
    kv = (rmsnorm(x, g_kv) @ w_kv).reshape(b, t, N_DIL, 2, N_KV_B, HEAD_DIM)
    k = rmsnorm(kv[:, :, :, 0], k_norm[:, None, :])
    k = rope(k.reshape(b, t, N_DIL * N_KV_B, HEAD_DIM), pos).reshape(b, t, N_DIL, N_KV_B, HEAD_DIM)
    return jnp.stack([k, kv[:, :, :, 1]], axis=3)

def b_queries(h, w_q, q_norm, pos):
    b, t, _ = h.shape
    q = rmsnorm((h @ w_q).reshape(b, t, N_DIL, N_HEADS_B, HEAD_DIM), q_norm[:, None, :])
    return rope(q.reshape(b, t, N_DIL * N_HEADS_B, HEAD_DIM), pos).reshape(b, t, N_DIL, N_HEADS_B, HEAD_DIM)

def hmoe(h, w_rg, b_rg, w_re, b_re, w_g, w_u, w_d):
    t = h.shape[0]
    hf = h.astype(jnp.float32)
    g_prob = jax.nn.softmax(hf @ w_rg.astype(jnp.float32) + b_rg.astype(jnp.float32), axis=-1)
    g_idx = jnp.argmax(g_prob, axis=-1)
    g_gate = jnp.max(g_prob, axis=-1)
    e_logits = (hf @ w_re.astype(jnp.float32) + b_re.astype(jnp.float32)).reshape(t, N_GROUPS, EXPERTS_PER_GROUP)
    e_logits = jnp.take_along_axis(e_logits, jnp.broadcast_to(g_idx[:, None, None], (t, 1, EXPERTS_PER_GROUP)), axis=1)[:, 0]
    top_p, top_i = lax.top_k(jax.nn.softmax(e_logits, axis=-1), TOP_K)
    weights = g_gate[:, None] * top_p / jnp.sum(top_p, axis=-1, keepdims=True)
    expert = g_idx[:, None] * EXPERTS_PER_GROUP + top_i
    comb = jnp.einsum('tk,tke->te', weights, jax.nn.one_hot(expert, N_EXPERTS, dtype=jnp.float32)).astype(h.dtype)
    a = jnp.einsum('td,edf->tef', h, w_g)
    u = jnp.einsum('td,edf->tef', h, w_u)
    return jnp.einsum('tef,efd->td', jax.nn.silu(a) * u * comb[:, :, None], w_d)

def setup_inputs(seed: int = 0) -> dict:
    key = jax.random.key(seed)
    ks = jax.random.split(key, 25)
    f32 = jnp.float32

    def nrm(k, shape, scale):
        return jax.random.normal(k, shape, f32) * scale

    n_pages = PAST_LEN // PAGE_SIZE
    n_used = DEC_BATCH * n_pages
    n_pool = n_used + max(1, n_used // 4)
    page_table = jax.random.permutation(ks[0], n_pool)[:n_used].reshape(DEC_BATCH, n_pages).astype(jnp.int32)
    lb = [min(w, PAST_LEN) for w, _ in DILATED]
    sb_bias = -jnp.linspace(SB_BIAS_MIN, SB_BIAS_MAX, N_HEADS_A, dtype=f32)[None, :] + nrm(ks[24], (N_A_LAYERS, N_HEADS_A), 0.1)
    return {
        "x_prompt": nrm(ks[1], (BATCH, SEQ, D_MODEL), 1.0),
        "x_sample": nrm(ks[2], (DEC_BATCH, DEC_SEQ, D_MODEL), 1.0),
        "cache_kv_a": nrm(ks[3], (N_A_LAYERS, n_pool, PAGE_SIZE, 2, N_HEADS_A, HEAD_DIM), 1.0),
        "cache_kv_b1": nrm(ks[4], (DEC_BATCH, lb[0], 2, N_KV_B, HEAD_DIM), 1.0),
        "cache_kv_b2": nrm(ks[5], (DEC_BATCH, lb[1], 2, N_KV_B, HEAD_DIM), 1.0),
        "cache_kv_b3": nrm(ks[6], (DEC_BATCH, lb[2], 2, N_KV_B, HEAD_DIM), 1.0),
        "page_table": page_table,
        "g_attn": 1.0 + nrm(ks[7], (DEPTH, D_MODEL), 0.05),
        "g_ffn": 1.0 + nrm(ks[8], (DEPTH, D_MODEL), 0.05),
        "w_qkv_a": nrm(ks[9], (N_A_LAYERS, D_MODEL, 3 * N_HEADS_A * HEAD_DIM), D_MODEL ** -0.5),
        "w_o_a": nrm(ks[10], (N_A_LAYERS, N_HEADS_A * HEAD_DIM, D_MODEL), (N_HEADS_A * HEAD_DIM) ** -0.5),
        "sb_bias": sb_bias,
        "g_kv": 1.0 + nrm(ks[11], (D_MODEL,), 0.05),
        "w_kv_b": nrm(ks[12], (D_MODEL, N_DIL * 2 * N_KV_B * HEAD_DIM), D_MODEL ** -0.5),
        "k_norm_b": 1.0 + nrm(ks[13], (N_DIL, HEAD_DIM), 0.05),
        "w_q_b": nrm(ks[14], (N_B_LAYERS, D_MODEL, N_DIL * N_HEADS_B * HEAD_DIM), D_MODEL ** -0.5),
        "q_norm_b": 1.0 + nrm(ks[15], (N_B_LAYERS, N_DIL, HEAD_DIM), 0.05),
        "w_o_b": nrm(ks[16], (N_B_LAYERS, N_HEADS_B * HEAD_DIM, D_MODEL), (N_HEADS_B * HEAD_DIM) ** -0.5),
        "w_router_group": nrm(ks[17], (DEPTH, D_MODEL, N_GROUPS), D_MODEL ** -0.5),
        "b_router_group": nrm(ks[18], (DEPTH, N_GROUPS), 0.01),
        "w_router_expert": nrm(ks[19], (DEPTH, D_MODEL, N_EXPERTS), D_MODEL ** -0.5),
        "b_router_expert": nrm(ks[20], (DEPTH, N_EXPERTS), 0.01),
        "w_gate": nrm(ks[21], (DEPTH, N_EXPERTS, D_MODEL, D_EXPERT), D_MODEL ** -0.5),
        "w_up": nrm(ks[22], (DEPTH, N_EXPERTS, D_MODEL, D_EXPERT), D_MODEL ** -0.5),
        "w_down": nrm(ks[23], (DEPTH, N_EXPERTS, D_EXPERT, D_MODEL), D_EXPERT ** -0.5),
    }

def reference(x_prompt, x_sample, cache_kv_a, cache_kv_b1, cache_kv_b2, cache_kv_b3, page_table,
              g_attn, g_ffn, w_qkv_a, w_o_a, sb_bias, g_kv, w_kv_b, k_norm_b, w_q_b, q_norm_b, w_o_b,
              w_router_group, b_router_group, w_router_expert, b_router_expert, w_gate, w_up, w_down):
    b, s, d = x_prompt.shape
    db, t, _ = x_sample.shape
    past_len = page_table.shape[1] * cache_kv_a.shape[2]
    pos_p = jnp.arange(s)
    pos_s = past_len + jnp.arange(t)
    buffers = (cache_kv_b1, cache_kv_b2, cache_kv_b3)
    xp, xs = x_prompt, x_sample
    new_a_p, new_a_s = [], []
    for layer in range(DEPTH):
        if layer < N_A_LAYERS:
            i = layer
            qkv = (rmsnorm(xp, g_attn[layer]) @ w_qkv_a[i]).reshape(b, s, 3, N_HEADS_A, HEAD_DIM)
            o_p = sb_prompt(qkv[:, :, 0], qkv[:, :, 1], qkv[:, :, 2], sb_bias[i])
            xp = xp + o_p.reshape(b, s, -1) @ w_o_a[i]
            new_a_p.append(qkv[:, :, 1:])
            qkv_s = (rmsnorm(xs, g_attn[layer]) @ w_qkv_a[i]).reshape(db, t, 3, N_HEADS_A, HEAD_DIM)
            past = cache_kv_a[i][page_table].reshape(db, past_len, 2, N_HEADS_A, HEAD_DIM)
            k_all = jnp.concatenate([past[:, :, 0], qkv_s[:, :, 1]], axis=1)
            v_all = jnp.concatenate([past[:, :, 1], qkv_s[:, :, 2]], axis=1)
            o_s = sb_attend(qkv_s[:, :, 0], k_all, v_all, pos_s, jnp.arange(past_len + t), sb_bias[i])
            xs = xs + o_s.reshape(db, t, -1) @ w_o_a[i]
            new_a_s.append(qkv_s[:, :, 1:])
        else:
            j = layer - N_A_LAYERS
            if j == 0:
                kv_p = shared_kv(xp, g_kv, w_kv_b, k_norm_b, pos_p)
                kv_s = shared_kv(xs, g_kv, w_kv_b, k_norm_b, pos_s)
            q_p = b_queries(rmsnorm(xp, g_attn[layer]), w_q_b[j], q_norm_b[j], pos_p)
            q_s = b_queries(rmsnorm(xs, g_attn[layer]), w_q_b[j], q_norm_b[j], pos_s)
            outs_p, lses_p, outs_s, lses_s = [], [], [], []
            for g, (window, dil) in enumerate(DILATED):
                o, l = dilated_prompt(q_p[:, :, g], kv_p[:, :, g, 0], kv_p[:, :, g, 1], window, dil)
                outs_p.append(o)
                lses_p.append(l)
                o, l = dilated_sample(q_s[:, :, g], buffers[g], kv_s[:, :, g], window, dil)
                outs_s.append(o)
                lses_s.append(l)
            xp = xp + combine_groups(outs_p, lses_p).reshape(b, s, -1) @ w_o_b[j]
            xs = xs + combine_groups(outs_s, lses_s).reshape(db, t, -1) @ w_o_b[j]
        moe = (w_router_group[layer], b_router_group[layer], w_router_expert[layer], b_router_expert[layer],
               w_gate[layer], w_up[layer], w_down[layer])
        xp = xp + hmoe(rmsnorm(xp, g_ffn[layer]).reshape(b * s, d), *moe).reshape(b, s, d)
        xs = xs + hmoe(rmsnorm(xs, g_ffn[layer]).reshape(db * t, d), *moe).reshape(db, t, d)
    new_kv_a_prompt = jnp.stack(new_a_p)
    new_kv_a_sample = jnp.stack(new_a_s)
    new_kv_b1_prompt = kv_p[:, s - min(DILATED[0][0], s):, 0]
    new_kv_b2_prompt = kv_p[:, s - min(DILATED[1][0], s):, 1]
    new_kv_b3_prompt = kv_p[:, s - min(DILATED[2][0], s):, 2]
    new_kv_b1_sample = kv_s[:, :, 0]
    new_kv_b2_sample = kv_s[:, :, 1]
    new_kv_b3_sample = kv_s[:, :, 2]
    return (xp, xs, new_kv_a_prompt, new_kv_a_sample, new_kv_b1_prompt, new_kv_b1_sample,
            new_kv_b2_prompt, new_kv_b2_sample, new_kv_b3_prompt, new_kv_b3_sample)


_drawn_inputs = setup_inputs


def setup_inputs(seed=0):
    import zlib

    import numpy as np

    out = dict(_drawn_inputs(seed))
    spreads = {}
    factors = {'q_norm_b': 4.218, 'b_router_group': 3.779, 'b_router_expert': 2.732}
    for name, (base, spread) in spreads.items():
        noise = np.random.default_rng([zlib.crc32(name.encode()), seed]).standard_normal(out[name].shape)
        drawn = base * np.exp(spread * noise) if base else spread * noise
        out[name] = __import__('jax').numpy.asarray(drawn.astype(out[name].dtype))
    for name, factor in factors.items():
        out[name] = (out[name] * factor).astype(out[name].dtype)
    return out
```

```python
from contextlib import ExitStack, contextmanager

import numpy as np

import concourse.bass as bass
from concourse import mybir

F32 = mybir.dt.float32
I32 = mybir.dt.int32
ALU = mybir.AluOpType
ACT = mybir.ActivationFunctionType
AX_X = mybir.AxisListType.X
ds = bass.ds

D = 1024
SEQ, DEC = 512, 8
TOK = SEQ + DEC
HALF = TOK // 2
TILES = [(t, 128) for t in range(SEQ // 128)] + [(SEQ // 128, DEC)]
NT = len(TILES)
KT = D // 128
HD = 64
NH = D // HD
NPAIR = NH // 2
PAST, PAGE = 256, 128
NCH = PAST // PAGE
SCALE = HD ** -0.5
EPS = 1e-6
NEG = -1e30
NKV = NH // 4
NDIL = 3
KQ = 5 * HD
NG, NE, EPG = 4, 32, 8
FE = D // 4
CAP = 64
NOVER = 2 * TOK // CAP
NSLOT = (NE + NOVER) * CAP
WSLOTS = 4

CONST = {}
_at = 0
for _name, _width in (("ident", 128), ("tri", 128), ("strict", 128), ("ones", 128),
                      ("cos", NT * 8), ("sin", NT * 8), ("valid", NT), ("iota", NE), ("iota99", NE),
                      ("ecap", NE), ("m0", 4 * 256), ("m1", 128), ("m2", 128), ("m3", 128), ("pidx", 1), ("eps", 1), ("eps64", NT), ("mhalf", NT)):
    CONST[_name] = (_at, _at + _width)
    _at += _width
NCONST = _at
S1ROWS = PAST // 4 + 1 + PAST // 16 + 1 + 1


def constants():
    c = np.zeros((128, NCONST), np.float32)

    def put(name, a):
        lo, hi = CONST[name]
        c[:, lo:hi] = np.asarray(a, np.float32).reshape(128, -1)

    p = np.arange(128)[:, None]
    m = np.arange(128)[None, :]
    put("ident", p == m)
    put("tri", p >= m)
    put("strict", p < m)
    put("ones", np.ones((128, 128)))
    pos = np.stack([np.arange(128) + 128 * t for t in range(NT)], 1).astype(np.float32)
    pos[:, NT - 1] = PAST
    half = HD // 8
    inv = np.power(np.float32(500000.0), -np.arange(half, dtype=np.float32) * np.float32(2.0) / np.float32(HD // 4))
    ang = (pos[:, :, None] * inv[None, None, :].astype(np.float32)).astype(np.float32)
    put("cos", np.cos(ang))
    put("sin", np.sin(ang))
    put("valid", np.stack([np.arange(128) < rows for _, rows in TILES], 1))
    put("iota", np.broadcast_to(np.arange(NE), (128, NE)))
    put("iota99", np.broadcast_to(np.arange(NE) + 99, (128, NE)))
    put("ecap", np.broadcast_to(np.arange(NE) * CAP, (128, NE)))
    m0 = np.full((128, 4, 256), NEG, np.float32)
    for b in range(4):
        if b:
            m0[:, b, 0:128] = np.where(m >= p, 0, NEG)
        m0[:, b, 128:256] = np.where(m <= p, 0, NEG)
    put("m0", m0)
    put("m1", np.where(m <= p, 0, NEG))
    put("m2", np.where((m <= p) & ((p - m) % 4 == 0), 0, NEG))
    put("m3", np.where(m > p, 0, NEG))
    put("pidx", 2 * np.arange(128))
    put("eps", np.full(128, EPS))
    put("eps64", np.full((128, NT), HD * EPS))
    put("mhalf", np.full((128, NT), -0.5))
    return c


def selectors():
    s = np.zeros((NDIL, DEC, DEC, S1ROWS), np.float32)
    n1, n2 = PAST // 4 + 1, PAST // 16 + 1
    for b in range(DEC):
        s[1, b, b, 0:n1] = 1
        s[2, b, b, n1:n1 + n2] = 1
        s[0, b, b, n1 + n2:] = 1
    return s.reshape(NDIL * DEC, -1)


class Steps:

    def __init__(self, sem):
        self.sem, self.total, self.n, self.base = sem, 0, 0, 0

    def on(self, eng):
        self.eng = eng

    def enter(self, i, per):
        self.base, self.n, self.per = self.total + i * per, 0, per

    def leave(self, count):
        assert self.n == self.per, (self.sem, self.n, self.per)
        self.total += count * self.per
        self.base, self.n = self.total, 0

    def done(self):
        self.total = self.base + self.n
        self.base, self.n = self.total, 0

    def __call__(self, ins):
        ins.then_inc(self.sem, 1)
        self.n += 1
        self.eng.wait_ge(self.sem, self.base + self.n)


def flat(ap):
    return ap.rearrange("p a b -> p (a b)")


def build(nc, a, outs, stop=None):
    (y_prompt, y_sample, a_prompt, a_sample, b1p, b1s, b2p, b2s, b3p, b3s) = outs
    kv_out = ((b1p, b1s, 128), (b2p, b2s, SEQ), (b3p, b3s, SEQ))
    xs_rows = nc.dram_tensor("xs_rows", [NSLOT, D], F32, kind="Internal").ap()
    ys_rows = nc.dram_tensor("ys_rows", [NSLOT, D], F32, kind="Internal").ap()
    o_rows = [nc.dram_tensor(f"o_rows{g}", [SEQ, 4 * 66], F32, kind="Internal").ap() for g in range(2)]

    s_rows = nc.dram_tensor("s_rows", [NDIL, DEC, NKV, HD + KQ], F32, kind="Internal").ap()

    with ExitStack() as ctx:
        def sb(name, shape, dt=F32, to=ctx):
            return to.enter_context(nc.sbuf_tensor(name, shape, dt))

        live = [[]]

        def sem(name):
            live[-1].append(nc.alloc_semaphore(name=name))
            return live[-1][-1]

        def scoped(stage):
            def run(*args, **kw):
                live.append([])
                stage(*args, **kw)
                nc.clear_and_free_semaphores(live.pop())
                nc.all_engine_barrier()
            return run

        ps = ctx.enter_context(nc.psum_tensor("ps", [128, 8 * 512], F32))

        def bank(b, n=1):
            return ps[:, 512 * b:512 * (b + n)]

        cst = sb("cst", [128, NCONST])
        x = sb("x", [128, NT, D])
        oT = sb("oT", [128, NPAIR, TOK])

        def C(name):
            return cst[:, CONST[name][0]:CONST[name][1]]

        ident, ones = C("ident"), C("ones")
        s_act, s_dve, s_pool = sem("act_steps"), sem("dve_steps"), sem("pool_steps")
        act_do, dve_do, pool_do = Steps(s_act), Steps(s_dve), Steps(s_pool)
        s_const, s_x, s_zero, s_zeroed = sem("const_in"), sem("x_in"), sem("zero_tile"), sem("xs_zeroed")

        zero = sb("zero", [128, D])
        with nc.Block() as block:
            @block.sync
            def _(sp):
                sp.dma_start(cst[:, :], a["const"]).then_inc(s_const, 16)
                sp.dma_start(x[:, 0:4, :], a["x_prompt"][0].rearrange("(t p) d -> p t d", p=128)).then_inc(s_x, 16)
                sp.dma_start(x[0:DEC, 4, :], a["x_sample"][:, 0, :]).then_inc(s_x, 16)
                sp.wait_ge(s_const, 16)
                sp.wait_ge(s_x, 32)

            @block.vector
            def _(dve):
                dve.memset(zero[:, :], 0.0).then_inc(s_zero, 1)

        norm_no = [0]

        @scoped
        def norm_phase(gains, outs_T, keep=None, prefetch=None):
            k = norm_no[0]
            norm_no[0] += 1
            s_g, s_rstd, s_xn, s_tp, s_ev = (sem(f"{n}{k}") for n in
                                             ("gain_in", "rstd_ready", "xn_ready", "xn_turned", "xnT_ready"))
            with ExitStack() as ph, nc.Block() as block:
                gb = sb(f"gb{k}", [128, len(gains), D], to=ph)
                xn = keep if keep is not None else sb(f"xn{k}", [128, 2, D], to=ph)
                junk = sb(f"junk{k}", [128, D], to=ph)
                ss = sb(f"ss{k}", [128, NT], to=ph)
                rs = sb(f"rs{k}", [128, NT], to=ph)
                units = [(t, rows, gi) for t, rows in TILES for gi in range(len(gains))]

                def slot(n, t):
                    return t if keep is not None else n % 2

                @block.sync
                def _(sp):
                    for gi, g in enumerate(gains):
                        sp.dma_start(gb[:, gi, :], g.partition_broadcast(128)).then_inc(s_g, 16)
                    if prefetch:
                        prefetch(sp)

                @block.scalar
                def _(act):
                    act_do.on(act)
                    for t, rows in TILES:
                        act_do(nc.scalar.activation(junk[0:rows, :], x[0:rows, t, :], ACT.Square,
                                                    accum_out=ss[0:rows, t:t + 1]))
                        act_do(nc.scalar.activation(rs[0:rows, t:t + 1], ss[0:rows, t:t + 1], ACT.Ln,
                                                    bias=C("eps")[0:rows, :], scale=1.0 / D))
                        nc.scalar.activation(rs[0:rows, t:t + 1], rs[0:rows, t:t + 1], ACT.Exp,
                                             scale=-0.5).then_inc(s_rstd, 1)
                    act_do.done()
                    for n, (t, rows, gi) in enumerate(units):
                        act.wait_ge(s_tp, n + 1)
                        src = bank(2 * (n % 2), 2).rearrange("p (k m) -> p k m", k=KT)
                        nc.scalar.activation(outs_T[gi][:, :, 128 * t:128 * t + rows], src[:, :, 0:rows],
                                             ACT.Copy).then_inc(s_ev, 1)

                @block.vector
                def _(dve):
                    dve.wait_ge(s_g, 16 * len(gains))
                    for n, (t, rows, gi) in enumerate(units):
                        dve.wait_ge(s_rstd, t + 1)
                        if keep is None and n >= 2:
                            dve.wait_ge(s_tp, n - 1)
                        nc.vector.scalar_tensor_tensor(
                            out=xn[0:rows, slot(n, t), :], in0=x[0:rows, t, :], scalar=rs[0:rows, t:t + 1],
                            in1=gb[0:rows, gi, :], op0=ALU.mult, op1=ALU.mult).then_inc(s_xn, 1)

                @block.tensor
                def _(pe):
                    for n, (t, rows, gi) in enumerate(units):
                        pe.wait_ge(s_xn, n + 1)
                        if n >= 2:
                            pe.wait_ge(s_ev, n - 1)
                        dst = bank(2 * (n % 2), 2).rearrange("p (k m) -> p k m", k=KT)
                        for kt in range(KT):
                            last = nc.tensor.transpose(dst[:, kt, 0:rows],
                                                       xn[0:rows, slot(n, t), kt:D:KT], ident[0:rows, 0:rows])
                        last.then_inc(s_tp, 1)

        phA = ExitStack()
        xnT = sb("xnT_a", [128, KT, TOK], to=phA)
        norm_phase([a["g_attn"][0]], [xnT])
        qTs = sb("qTs", [128, NPAIR, DEC], to=phA)
        vres = sb("vres", [128, DEC * NCH, D], to=phA)
        s_vres = sem("past_v_in")
        gidx = sb("gidx", [128, 2, DEC * NCH], I32, to=phA)
        w_qkv = a["w_qkv_a"][0].rearrange("(p t) n -> p t n", t=KT)
        cache_rows = a["cache_kv_a"][0].rearrange("g s c h e -> (g s c) (h e)")
        OFF = {0: 0, 1: 512, 3: 896, 2: 1024}
        NZ = 1280

        with ExitStack() as ph, nc.Block() as block:
            wA = sb("wA", [128, 3, KT, 128], to=ph)
            qkvT = sb("qkvT", [128, 3, TOK], to=ph)
            kv_tok = sb("kv_tok", [128, 2, NT, 128], to=ph)
            bias = sb("bias", [128, NH], to=ph)
            z = sb("z", [128, 2, NZ], to=ph)
            w = sb("w", [128, 2, NZ], to=ph)
            spl = sb("spl", [128, 2, NZ], to=ph)
            U = sb("U", [128, 2, 384], to=ph)
            ptab = sb("ptab", [128, DEC * NCH], I32, to=ph)
            ptf = sb("ptf", [128, 2, DEC * NCH], to=ph)
            s_w = [sem(f"w_{n}_in") for n in "qkv"]
            s_bias, s_pt, s_idx = sem("bias_in"), sem("pages_in"), sem("row_index_ready")
            s_proj, s_pev, s_qk, s_zev = sem("proj_done"), sem("proj_copied"), sem("scores_done"), sem("z_ready")
            s_abs, s_log, s_sp, s_spm = sem("abs_ready"), sem("log_ready"), sem("softplus_ready"), sem("softplus_masked")
            s_c, s_t, s_tm, s_a = sem("tails_done"), sem("logw_ready"), sem("logw_masked"), sem("weights_ready")
            s_av, s_oev, s_kvt, s_kve, s_kvo = (sem("av_done"), sem("av_copied"), sem("kv_turned"),
                                                sem("kv_tok_ready"), sem("kv_stored"))
            s_qs = sem("sample_q_kept")

            @block.sync
            def _(sp):
                sp.dma_start(bias[:, :], a["sb_bias"][0].partition_broadcast(128)).then_inc(s_bias, 16)
                sp.dma_start(ptab[:, :], a["page_table"].rearrange("b c -> (b c)").partition_broadcast(128)).then_inc(s_pt, 16)
                for m in range(3):
                    sp.dma_start(wA[:, m], w_qkv[:, :, m * D:m * D + 128]).then_inc(s_w[m], 16)

                def body(n, last):
                    if not last:
                        for m in range(3):
                            sp.wait_ge(s_proj, 3 * n + m + 1)
                            sp.dma_start(wA[:, m], w_qkv[:, :, ds(m * D + 128 * (n + 1), 128)]).then_inc(s_w[m], 16)
                    sp.wait_ge(s_kve, 4 * n + 4)
                    for c in range(2):
                        dst_p = a_prompt[0, 0].rearrange("(t p) c h e -> p t c (h e)", p=128)
                        sp.dma_start(dst_p[:, :, c, ds(128 * n, 128)], kv_tok[:, c, 0:4, :]).then_inc(s_kvo, 16)
                        dst_s = a_sample[0, :, 0].rearrange("b c h e -> b c (h e)")
                        sp.dma_start(dst_s[:, c, ds(128 * n, 128)], kv_tok[0:DEC, c, 4, :]).then_inc(s_kvo, 16)

                with sp.Fori(0, NPAIR - 1) as n:
                    body(n, False)
                body(NPAIR - 1, True)
                sp.wait_ge(s_kvo, 64 * NPAIR)

            def project(pe, m, n):
                pe.wait_ge(s_w[m], 16 * n + 16)
                if m:
                    pe.wait_ge(s_pev, 3 * n + m)
                else:
                    pe.wait_ge(s_kve, 4 * n)
                    pe.wait_ge(s_pev, 3 * n)
                for h in range(2):
                    for k in range(KT):
                        last = nc.tensor.matmul(bank(6 + h)[:, 0:HALF], wA[:, m, k, :],
                                                xnT[:, k, HALF * h:HALF * h + HALF],
                                                start=(k == 0), stop=(k == KT - 1))
                last.then_inc(s_proj, 1)

            def turn_kv(pe, n):
                pe.wait_ge(s_pev, 3 * n + 3)
                for c in range(2):
                    if c:
                        pe.wait_ge(s_kve, 4 * n + 2)
                    for t, rows in TILES:
                        last = nc.tensor.transpose(ps[0:rows, 512 * 6 + 128 * t:512 * 6 + 128 * t + 128],
                                                   qkvT[:, 1 + c, 128 * t:128 * t + rows], ident)
                    last.then_inc(s_kvt, 1)

            @block.tensor
            def _(pe):
                for m in range(3):
                    project(pe, m, 0)
                turn_kv(pe, 0)

                def body(n, last_pair):
                    for h in range(2):
                        r = slice(64 * h, 64 * h + 64)
                        for c in range(4):
                            o = 1536 * h + OFF[c]
                            last = nc.tensor.matmul(ps[:, o:o + 512 - 128 * c], qkvT[r, 1, 128 * c:128 * c + 128],
                                                    qkvT[r, 0, 128 * c:512], start=True, stop=True)
                        last.then_inc(s_qk, 1)
                    if not last_pair:
                        project(pe, 0, n + 1)
                        project(pe, 1, n + 1)
                    for h in range(2):
                        pe.wait_ge(s_spm, 2 * n + h + 1)
                        b = 1536 * h

                        def mm(lhs, rhs, o, start, stop, width):
                            return nc.tensor.matmul(ps[:, b + o:b + o + width], lhs, rhs, start=start, stop=stop,
                                                    skip_group_check=True)

                        S = spl[:, h, :]
                        tri = C("tri")
                        mm(tri, S[:, 0:512], 0, True, False, 512)
                        mm(ones, S[:, 512:640], 128, False, False, 128)
                        mm(ones, U[:, h, 128:384], 256, False, True, 256)
                        mm(tri, S[:, 512:896], 512, True, False, 384)
                        mm(ones, S[:, 1024:1152], 640, False, False, 128)
                        mm(ones, U[:, h, 0:128], 768, False, True, 128)
                        mm(tri, S[:, 896:1024], 896, True, True, 128)
                        mm(tri, S[:, 1024:1280], 1024, True, False, 256)
                        mm(ones, S[:, 896:1024], 1152, False, True, 128).then_inc(s_c, 1)
                    if not last_pair:
                        project(pe, 2, n + 1)
                    for h in range(2):
                        pe.wait_ge(s_a, 2 * n + h + 1)
                        for c in range(4):
                            last = nc.tensor.matmul(ps[64 * h:64 * h + 64, 128 * c:512],
                                                    kv_tok[:, 1, c, 64 * h:64 * h + 64],
                                                    w[:, h, OFF[c]:OFF[c] + 512 - 128 * c],
                                                    start=(c == 0), stop=(c == 3), skip_group_check=True)
                    last.then_inc(s_av, 1)
                    if not last_pair:
                        turn_kv(pe, n + 1)
                        pe.wait_ge(s_t, 2 * n + 2)
                        pe.wait_ge(s_oev, n + 1)

                with pe.Fori(0, NPAIR - 1) as n:
                    body(n, False)
                body(NPAIR - 1, True)

            @block.scalar
            def _(act):
                act_do.on(act)

                def proj_copy(m, n):
                    act.wait_ge(s_proj, 3 * n + m + 1)
                    if m == 0:
                        act.wait_ge(s_qs, n)
                    src = bank(6, 2).rearrange("p (h m) -> p h m", h=2)[:, :, 0:HALF]
                    nc.scalar.activation(qkvT[:, m, :].rearrange("p (h m) -> p h m", h=2), src,
                                         ACT.Copy).then_inc(s_pev, 1)

                for m in range(3):
                    proj_copy(m, 0)
                act.wait_ge(s_bias, 16)

                def body(n, last_pair):
                    for h in range(2):
                        act.wait_ge(s_qk, 2 * n + h + 1)
                        nc.scalar.activation(z[:, h, :], ps[:, 1536 * h:1536 * h + NZ], ACT.Identity,
                                             bias=bias[:, ds(2 * n + h, 1)], scale=SCALE).then_inc(s_zev, 1)
                    for h in range(2):
                        act.wait_ge(s_abs, 2 * n + h + 1)
                        act_do(nc.scalar.activation(w[:, h, :], w[:, h, :], ACT.Exp))
                        nc.scalar.activation(w[:, h, :], w[:, h, :], ACT.Ln, bias=1.0).then_inc(s_log, 1)
                    if not last_pair:
                        proj_copy(0, n + 1)
                        proj_copy(1, n + 1)
                    for h in range(2):
                        act.wait_ge(s_tm, 2 * n + h + 1)
                        nc.scalar.activation(w[:, h, :], w[:, h, :], ACT.Exp).then_inc(s_a, 1)
                    if not last_pair:
                        proj_copy(2, n + 1)

                with act.Fori(0, NPAIR - 1) as n:
                    act_do.enter(n, 2)
                    body(n, False)
                act_do.leave(NPAIR - 1)
                act_do.enter(0, 2)
                body(NPAIR - 1, True)
                act_do.leave(1)

            @block.vector
            def _(dve):
                dve_do.on(dve)
                dve.wait_ge(s_pt, 16)
                dve_do(nc.vector.tensor_copy(ptf[:, 0, :], ptab[:, :]))
                dve_do(nc.vector.tensor_scalar(ptf[:, 0, :], ptf[:, 0, :], 2.0 * PAGE, C("pidx"), ALU.mult, ALU.add))
                dve_do(nc.vector.tensor_scalar(ptf[:, 1, :], ptf[:, 0, :], 1.0, None, ALU.add))
                nc.vector.tensor_copy(gidx[:, :, :], ptf[:, :, :]).then_inc(s_idx, 1)
                dve_do.done()

                def kv_copy(n):
                    dve.wait_ge(s_kvo, 64 * n)
                    for c in range(2):
                        dve.wait_ge(s_kvt, 2 * n + c + 1)
                        nc.vector.tensor_copy(flat(kv_tok[:, c, 0:4, :]), bank(6)).then_inc(s_kve, 1)
                        nc.vector.tensor_copy(kv_tok[0:DEC, c, 4, :], bank(7)[0:DEC, 0:128]).then_inc(s_kve, 1)

                def q_keep(n):
                    dve.wait_ge(s_pev, 3 * n + 1)
                    nc.vector.tensor_copy(qTs[:, ds(n, 1), :], qkvT[:, 0:1, SEQ:TOK]).then_inc(s_qs, 1)

                q_keep(0)
                kv_copy(0)

                def body(n, last_pair):
                    for h in range(2):
                        dve.wait_ge(s_zev, 2 * n + h + 1)
                        nc.vector.scalar_tensor_tensor(out=w[:, h, :], in0=z[:, h, :], scalar=-1.0, in1=z[:, h, :],
                                                       op0=ALU.mult, op1=ALU.min).then_inc(s_abs, 1)
                    for h in range(2):
                        dve.wait_ge(s_log, 2 * n + h + 1)
                        nc.vector.scalar_tensor_tensor(out=spl[:, h, :], in0=z[:, h, :], scalar=0.0, in1=w[:, h, :],
                                                       op0=ALU.max, op1=ALU.add).then_inc(s_sp, 1)
                    if not last_pair:
                        q_keep(n + 1)
                    for h in range(2):
                        dve.wait_ge(s_c, 2 * n + h + 1)
                        nc.vector.tensor_tensor(w[:, h, :], z[:, h, :], ps[:, 1536 * h:1536 * h + NZ],
                                                ALU.subtract).then_inc(s_t, 1)
                    dve.wait_ge(s_av, n + 1)
                    nc.vector.tensor_copy(oT[:, ds(n, 1), 0:512],
                                          bank(0).rearrange("p (a m) -> p a m", a=1)).then_inc(s_oev, 1)
                    if not last_pair:
                        kv_copy(n + 1)

                with dve.Fori(0, NPAIR - 1) as n:
                    body(n, False)
                body(NPAIR - 1, True)

            @block.gpsimd
            def _(pool):
                pool_do.on(pool)
                pool.wait_ge(s_idx, 1)
                for u in range(DEC * NCH):
                    pool.indirect_dma_start(out=vres[:, u, :], out_offset=None, in_=cache_rows,
                                            in_offset=bass.IndirectOffsetOnAxis(ap=gidx[:, 1, u:u + 1], axis=0)
                                            ).then_inc(s_vres, 16)

                def diagonal(t, mask, op):
                    for c in range(4):
                        v = t[:, OFF[c]:OFF[c] + 128]
                        last = nc.gpsimd.tensor_tensor(v, v, mask, op)
                        if c < 3:
                            pool_do(last)
                    return last

                def body(n):
                    for h in range(2):
                        pool.wait_ge(s_sp, 2 * n + h + 1)
                        S = spl[:, h, :]
                        pool_do(diagonal(S, C("strict"), ALU.mult))
                        pool_do(nc.gpsimd.tensor_tensor(U[:, h, 0:128], S[:, 1152:1280], S[:, 896:1024], ALU.add))
                        pool_do(nc.gpsimd.tensor_tensor(U[:, h, 128:256], S[:, 640:768], S[:, 1024:1152], ALU.add))
                        nc.gpsimd.tensor_tensor(U[:, h, 256:384], S[:, 768:896], U[:, h, 0:128],
                                                ALU.add).then_inc(s_spm, 1)
                    for h in range(2):
                        pool.wait_ge(s_t, 2 * n + h + 1)
                        diagonal(w[:, h, :], C("m3"), ALU.add).then_inc(s_tm, 1)

                with pool.Fori(0, NPAIR) as n:
                    pool_do.enter(n, 2 * 6 + 2 * 3)
                    body(n)
                pool_do.leave(NPAIR)

        class OutProjection:

            def __init__(self, name, w_o, ph):
                self.w_o = w_o
                self.w = sb(f"wo_{name}", [128, NPAIR, D], to=ph)
                self.s_in, self.s_done, self.s_added = sem(f"wo_in_{name}"), sem(f"oproj_done_{name}"), sem(f"x_added_{name}")

            def load(self, sp):
                for m in range(NPAIR):
                    sp.dma_start(self.w[:, m, :], self.w_o[128 * m:128 * m + 128, :]).then_inc(self.s_in, 16)

            def product(self, pe, i):
                t, n = i // 2, i % 2
                rows = TILES[t][1]
                if i == 0:
                    pe.wait_ge(self.s_in, 16 * NPAIR)
                if i >= 2:
                    pe.wait_ge(self.s_added, i - 1)
                for m in range(NPAIR):
                    last = nc.tensor.matmul(bank(6 + n)[0:rows, :], oT[:, m, 128 * t:128 * t + rows],
                                            self.w[:, m, 512 * n:512 * n + 512], start=(m == 0), stop=(m == NPAIR - 1))
                last.then_inc(self.s_done, 1)

            def add(self, dve, i):
                t, n = i // 2, i % 2
                rows = TILES[t][1]
                dve.wait_ge(self.s_done, i + 1)
                xh = x[0:rows, t, 512 * n:512 * n + 512]
                nc.vector.tensor_tensor(xh, xh, bank(6 + n)[0:rows, :], ALU.add).then_inc(self.s_added, 1)

        with ExitStack() as ph, nc.Block() as block:
            kpast = sb("kpast", [128, 3, D], to=ph)
            qrow = sb("qrow", [DEC, D], to=ph)
            prod = sb("prod", [128, D], to=ph)
            oh_a = sb("oh_a", [128, 2, D], to=ph)
            out_a = OutProjection("a", a["w_o_a"][0], ph)
            biasb = sb("biasb", [128, NH], to=ph)
            zs = sb("zs", [128, NCH, DEC, NH], to=ph)
            ws = sb("ws", [128, NCH * 128], to=ph)
            sps = sb("sps", [128, NCH * 128], to=ph)
            s_k = [sem(f"past_k_in{i}") for i in range(3)]
            s_b, s_qt, s_qr, s_qb, s_z, s_e, s_zz, s_lg, s_so, s_ct, s_lw, s_wt, s_pv, s_fin = (
                sem(n) for n in ("sbias_in", "sq_turned", "sq_rows", "sq_spread", "sz_done", "sprod_done", "sz_ready",
                                 "slog_ready", "ssoftplus", "stails", "slogw", "sweights", "spv_done", "so_ready"))
            s_oh0, s_ohc, s_ot = sem("sheads_zeroed"), sem("sheads_copied"), sem("sheads_turned")
            units = [(b, c) for b in range(DEC) for c in range(NCH)]

            @block.sync
            def _(sp):
                sp.dma_start(biasb[:, :], a["sb_bias"][0].partition_broadcast(128)).then_inc(s_b, 16)
                out_a.load(sp)
                sp.wait_ge(s_zero, 1)
                with sp.Fori(0, NSLOT // 128) as i:
                    sp.dma_start(xs_rows[ds(i * 128, 128), :], zero[:, :]).then_inc(s_zeroed, 16)
                with sp.Fori(NE * CAP // 128, NSLOT // 128) as i:
                    sp.dma_start(ys_rows[ds(i * 128, 128), :], zero[:, :]).then_inc(s_zeroed, 16)

            @block.gpsimd
            def _(pool):
                for u in range(len(units)):
                    if u >= 3:
                        pool.wait_ge(s_e, u - 2)
                    pool.indirect_dma_start(out=kpast[:, u % 3, :], out_offset=None, in_=cache_rows,
                                            in_offset=bass.IndirectOffsetOnAxis(ap=gidx[:, 0, u:u + 1], axis=0)
                                            ).then_inc(s_k[u % 3], 16)

            @block.tensor
            def _(pe):
                for k in range(NPAIR):
                    last = nc.tensor.transpose(ps[0:DEC, 128 * k:128 * k + 128], qTs[:, k, :], ident)
                last.then_inc(s_qt, 1)
                pe.wait_ge(s_qr, 1)
                for b in range(DEC):
                    if b >= 2:
                        pe.wait_ge(s_z, NCH * (b - 1))
                    for n in range(2):
                        last = nc.tensor.matmul(bank(2 + 2 * (b % 2) + n), ident[0:DEC, b:b + 1].to_broadcast([DEC, 128]),
                                                qrow[:, 512 * n:512 * n + 512], start=True, stop=True)
                    last.then_inc(s_qb, 1)
                    if b:
                        out_a.product(pe, b - 1)
                out_a.product(pe, DEC - 1)
                pe.wait_ge(s_so, 1)
                nc.tensor.matmul(bank(0)[:, 0:128], C("tri"), sps[:, 0:128], start=True, stop=False, skip_group_check=True)
                nc.tensor.matmul(bank(0)[:, 0:128], ones, sps[:, 128:256], start=False, stop=True, skip_group_check=True)
                nc.tensor.matmul(bank(0)[:, 128:256], C("tri"), sps[:, 128:256], start=True, stop=True,
                                 skip_group_check=True).then_inc(s_ct, 1)
                pe.wait_ge(s_wt, 1)
                pe.wait_ge(s_vres, 16 * len(units))
                wv = ws[:, :].rearrange("p (c b h) -> p c b h", c=NCH, b=DEC)
                for b in range(DEC):
                    for n in range(2):
                        for c in range(NCH):
                            last = nc.tensor.matmul(bank(2 + 2 * (b // 4) + n)[32 * (b % 4):32 * (b % 4) + NH, :], wv[:, c, b, :],
                                                    vres[:, NCH * b + c, 512 * n:512 * n + 512], start=(c == 0), stop=(c == NCH - 1))
                    if b % 4 == 3:
                        last.then_inc(s_pv, 1)
                for q in range(2):
                    pe.wait_ge(s_ohc, 8 * q + 8)
                    for h in range(NH):
                        o = 8 * (h // 2) + 4 * q
                        last = nc.tensor.matmul(bank(1)[64 * (h % 2):64 * (h % 2) + 64, o:o + 4], oh_a[:, q, HD * h:HD * h + HD],
                                                ident[:, h:128:32], start=True, stop=True)
                last.then_inc(s_ot, 1)
                pe.wait_ge(s_fin, 1)
                for i in (8, 9):
                    out_a.product(pe, i)

            @block.vector
            def _(dve):
                dve_do.on(dve)
                dve.wait_ge(s_qt, 1)
                nc.vector.tensor_copy(qrow[:, :], ps[0:DEC, 0:1024]).then_inc(s_qr, 1)
                nc.vector.memset(flat(oh_a), 0.0).then_inc(s_oh0, 1)
                for u, (b, c) in enumerate(units):
                    dve.wait_ge(s_k[u % 3], 16 * (u // 3 + 1))
                    dve.wait_ge(s_qb, b + 1)
                    nc.vector.tensor_tensor(prod[:, :], kpast[:, u % 3, :], bank(2 + 2 * (b % 2), 2), ALU.mult).then_inc(s_e, 1)
                    dve.wait_ge(s_e, u + 1)
                    nc.vector.reduce_sum(zs[:, c, b, :], prod[:, :].rearrange("p (h e) -> p h e", e=HD), AX_X).then_inc(s_z, 1)
                    dve.wait_ge(s_z, u + 1)
                    if c == NCH - 1 and b >= 1:
                        out_a.add(dve, b - 1)
                dve.wait_ge(s_b, 16)
                zf = zs[:, :, :, :].rearrange("p c b h -> p (c b) h")
                zw = zs[:, :, :, :].rearrange("p c b h -> p (c b h)")
                dve_do(nc.vector.tensor_scalar(zw, zw, SCALE, None, ALU.mult))
                dve_do(nc.vector.tensor_tensor(zf, zf, biasb[:, :].unsqueeze(1).to_broadcast([128, NCH * DEC, NH]), ALU.add))
                nc.vector.scalar_tensor_tensor(out=ws[:, :], in0=zw, scalar=-1.0, in1=zw, op0=ALU.mult,
                                               op1=ALU.min).then_inc(s_zz, 1)
                out_a.add(dve, DEC - 1)
                dve.wait_ge(s_lg, 1)
                nc.vector.scalar_tensor_tensor(out=sps[:, :], in0=zw, scalar=0.0, in1=ws[:, :], op0=ALU.max,
                                               op1=ALU.add).then_inc(s_so, 1)
                dve.wait_ge(s_ct, 1)
                nc.vector.tensor_tensor(ws[:, :], zw, bank(0)[:, 0:256], ALU.subtract).then_inc(s_lw, 1)
                dve.wait_ge(s_oh0, 1)
                for q in range(2):
                    dve.wait_ge(s_pv, q + 1)
                    for i in range(4):
                        for n in range(2):
                            rows = slice(32 * i, 32 * i + NH)
                            nc.vector.tensor_copy(oh_a[rows, q, 512 * n:512 * n + 512], bank(2 + 2 * q + n)[rows, :]).then_inc(s_ohc, 1)
                dve.wait_ge(s_ot, 1)
                nc.vector.tensor_copy(oT[:, :, SEQ:TOK], bank(1)[:, 0:DEC * NPAIR].rearrange("p (n b) -> p n b", b=DEC)).then_inc(s_fin, 1)
                for i in (8, 9):
                    out_a.add(dve, i)
                dve_do.done()

            @block.scalar
            def _(act):
                act_do.on(act)
                act.wait_ge(s_zz, 1)
                act_do(nc.scalar.activation(ws[:, :], ws[:, :], ACT.Exp))
                nc.scalar.activation(ws[:, :], ws[:, :], ACT.Ln, bias=1.0).then_inc(s_lg, 1)
                act.wait_ge(s_lw, 1)
                nc.scalar.activation(ws[:, :], ws[:, :], ACT.Exp).then_inc(s_wt, 1)
                act_do.done()
        phA.close()

        def open_ring(sp, sems):
            for s in sems:
                sp.nop().then_inc(s, 1)

        @scoped
        def moe(layer):
            L = str(layer)

            def lsem(n):
                return sem(f"{n}_{L}")

            pos_i = sb("pos_i" + L, [128, 2, NT], I32, to=phM)
            wts = sb("wts" + L, [128, 2, NT], to=phM)
            over_i = sb("over_i" + L, [1, NOVER + 1], I32, to=phM)
            s_disp = lsem("rows_placed")
            wg = [sb(f"wg{s}_" + L, [128, KT, FE], to=phM) for s in range(WSLOTS)]
            wu = [sb(f"wu{s}_" + L, [128, KT, FE], to=phM) for s in range(WSLOTS)]
            wd = [sb(f"wd{s}_" + L, [128, 2, D], to=phM) for s in range(WSLOTS)]
            s_in = [lsem(f"block_in{s}") for s in range(WSLOTS)]

            def load_weights(eng, s, e, sig):
                eng.dma_start(wg[s][:, :, :], a["w_gate"][layer, ds(e, 1)].rearrange("a (p t) f -> p (a t) f", t=KT)).then_inc(sig, 16)
                eng.dma_start(wu[s][:, :, :], a["w_up"][layer, ds(e, 1)].rearrange("a (p t) f -> p (a t) f", t=KT)).then_inc(sig, 16)
                eng.dma_start(wd[s][:, :, :], a["w_down"][layer, ds(e, 1)].rearrange("a (p t) d -> p (a t) d", t=2)).then_inc(sig, 16)

            def load_rows(eng, s, row0, sig):
                eng.dma_start(xs[s][:, :], xs_rows[ds(row0, CAP), :]).then_inc(sig, 16)

            def first_weights(sp):
                for s in range(WSLOTS):
                    load_weights(sp, s, s, s_in[s])

            with ExitStack() as ph:
                xn = sb("xn_m" + L, [128, NT, D], to=ph)
                xnT = sb("xnT_m" + L, [128, KT, TOK], to=ph)
                norm_phase([a["g_ffn"][layer]], [xnT], keep=xn, prefetch=first_weights)
                wr = sb("wr" + L, [128, KT, NG + NE], to=ph)
                rb = sb("rb" + L, [128, NG + NE], to=ph)
                lg = sb("lg" + L, [128, NT, NG + NE], to=ph)
                st = sb("st" + L, [128, 12, NT], to=ph)
                g4 = sb("g4" + L, [128, 3, NT, NG], to=ph)
                el = sb("el" + L, [128, NT, NE], to=ph)
                oh = sb("oh" + L, [128, 3, NT, NE], to=ph)
                tmp = sb("tmp" + L, [128, NT, NE], to=ph)
                rank = sb("rank" + L, [128, NT, NE], to=ph)
                nov = sb("nov" + L, [NE, 2, 128], to=ph)
                ovb = sb("ovb" + L, [128, NE + 1], to=ph)
                far = sb("far" + L, [128, NE], to=ph)
                ovm = sb("ovm" + L, [1, NOVER, NE], to=ph)
                ovf = sb("ovf" + L, [1, NOVER + 1], to=ph)
                s_r, s_l, s_ex, s_gx, s_oh, s_rk, s_nv, s_ob, s_pos = (
                    lsem(n) for n in ("router_in", "logits_done", "exp_in", "exp_ready", "onehot_ready", "ranks_done",
                                      "over_counted", "over_base", "slots_ready"))

                with nc.Block() as block:
                    @block.sync
                    def _(sp):
                        sp.dma_start(wr[:, :, 0:NG], a["w_router_group"][layer].rearrange("(p t) n -> p t n", t=KT)).then_inc(s_r, 16)
                        sp.dma_start(wr[:, :, NG:], a["w_router_expert"][layer].rearrange("(p t) n -> p t n", t=KT)).then_inc(s_r, 16)
                        sp.dma_start(rb[:, 0:NG], a["b_router_group"][layer].partition_broadcast(128)).then_inc(s_r, 16)
                        sp.dma_start(rb[:, NG:], a["b_router_expert"][layer].partition_broadcast(128)).then_inc(s_r, 16)

                    @block.tensor
                    def _(pe):
                        pe.wait_ge(s_r, 64)
                        for t, rows in TILES:
                            for k in range(KT):
                                last = nc.tensor.matmul(ps[0:rows, 64 * t:64 * t + NG + NE], xnT[:, k, 128 * t:128 * t + rows],
                                                        wr[:, k, :], start=(k == 0), stop=(k == KT - 1))
                        last.then_inc(s_l, 1)
                        pe.wait_ge(s_oh, 1)
                        for t in range(NT):
                            for u in range(t + 1):
                                nc.tensor.matmul(bank(1)[:, 32 * t:32 * t + 32], C("strict") if u == t else ones,
                                                 oh[:, 2, u, :], start=(u == 0), stop=(u == t))
                        for t in range(NT):
                            last = nc.tensor.matmul(bank(2)[0:NE, 0:128], oh[:, 2, t, :], ones, start=(t == 0), stop=(t == NT - 1))
                        last.then_inc(s_rk, 1)
                        pe.wait_ge(s_nv, 1)
                        nc.tensor.matmul(bank(3)[:, 0:NE + 1], nov[:, 1, :], C("strict")[0:NE, 0:NE + 1],
                                         start=True, stop=True).then_inc(s_ob, 1)

                    @block.scalar
                    def _(act):
                        act.wait_ge(s_ex, 1)
                        nc.scalar.activation(g4[:, 2], g4[:, 2], ACT.Exp).then_inc(s_gx, 1)
                        act.wait_ge(s_ex, 2)
                        nc.scalar.activation(st[:, 6, :], st[:, 6, :], ACT.Exp).then_inc(s_gx, 1)

                    @block.vector
                    def _(dve):
                        dve_do.on(dve)
                        V = nc.vector

                        def over(s, n):
                            return st[:, s, :].unsqueeze(2).to_broadcast([128, NT, n])

                        def row(name, n):
                            return C(name)[:, 0:n].unsqueeze(1).to_broadcast([128, NT, n])

                        def first(dst, src, n, mx, ix, eq):
                            dve_do(V.tensor_reduce(st[:, mx, :], src, AX_X, ALU.max))
                            dve_do(V.tensor_tensor(eq, src, over(mx, n), ALU.is_equal))
                            dve_do(V.scalar_tensor_tensor(out=eq, in0=eq, scalar=-99.0, in1=row("iota99", n),
                                                          op0=ALU.mult, op1=ALU.add))
                            dve_do(V.tensor_reduce(st[:, ix, :], eq, AX_X, ALU.min))
                            dve_do(V.tensor_tensor(dst, row("iota", n), over(ix, n), ALU.is_equal))

                        dve_do(V.memset(lg[:, :, :], 0.0))
                        dve.wait_ge(s_l, 1)
                        for t, rows in TILES:
                            dve_do(V.tensor_tensor(lg[0:rows, t, :], ps[0:rows, 64 * t:64 * t + NG + NE], rb[0:rows, :], ALU.add))
                        gl = lg[:, :, 0:NG]
                        first(g4[:, 0], gl, NG, 0, 1, g4[:, 1])
                        V.tensor_tensor(g4[:, 2], gl, over(0, NG), ALU.subtract).then_inc(s_ex, 1)
                        dve_do(V.tensor_scalar(g4[:, 1], g4[:, 0], -NEG, NEG, ALU.mult, ALU.add))
                        dve_do(V.tensor_tensor(el[:, :, :].rearrange("p t (g e) -> p t g e", g=NG),
                                               lg[:, :, NG:].rearrange("p t (g e) -> p t g e", g=NG),
                                               g4[:, 1].unsqueeze(3).to_broadcast([128, NT, NG, EPG]), ALU.add))
                        first(oh[:, 0], el[:, :, :], NE, 2, 3, tmp[:, :, :])
                        dve_do(V.scalar_tensor_tensor(out=el[:, :, :], in0=oh[:, 0], scalar=3 * NEG, in1=el[:, :, :],
                                                      op0=ALU.mult, op1=ALU.add))
                        first(oh[:, 1], el[:, :, :], NE, 4, 5, tmp[:, :, :])
                        V.tensor_tensor(st[:, 6, :], st[:, 4, :], st[:, 2, :], ALU.subtract).then_inc(s_ex, 1)
                        for k in range(2):
                            dve_do(V.tensor_tensor(oh[:, k], oh[:, k],
                                                   C("valid").unsqueeze(2).to_broadcast([128, NT, NE]), ALU.mult))
                        V.tensor_tensor(oh[:, 2], oh[:, 0], oh[:, 1], ALU.add).then_inc(s_oh, 1)
                        dve.wait_ge(s_gx, 2)
                        dve_do(V.reduce_sum(st[:, 7, :], g4[:, 2], AX_X))
                        dve_do(V.tensor_scalar(st[:, 8, :], st[:, 6, :], 1.0, None, ALU.add))
                        dve_do(V.tensor_tensor(st[:, 7, :], st[:, 7, :], st[:, 8, :], ALU.mult))
                        dve_do(V.reciprocal(wts[:, 0, :], st[:, 7, :]))
                        dve_do(V.tensor_tensor(wts[:, 1, :], wts[:, 0, :], st[:, 6, :], ALU.mult))
                        dve.wait_ge(s_rk, 1)
                        dve_do(V.tensor_copy(rank[:, :, :].rearrange("p t e -> p (t e)"), bank(1)[:, 0:NT * NE]))
                        dve_do(V.tensor_copy(nov[:, 0, :], bank(2)[0:NE, 0:128]))
                        dve_do(V.memset(nov[:, 1, :], 0.0))
                        blocks = -(-TOK // CAP)
                        for m in range(1, blocks):
                            ins = V.scalar_tensor_tensor(out=nov[:, 1, :], in0=nov[:, 0, :], scalar=float(CAP * m), in1=nov[:, 1, :],
                                                         op0=ALU.is_gt, op1=ALU.add)
                            if m < blocks - 1:
                                dve_do(ins)
                        ins.then_inc(s_nv, 1)
                        dve.wait_ge(s_ob, 1)
                        dve_do(V.tensor_copy(ovb[:, :], bank(3)[:, 0:NE + 1]))
                        dve_do(V.scalar_tensor_tensor(out=far[:, :], in0=ovb[:, 0:NE], scalar=float(CAP), in1=C("ecap"),
                                                      op0=ALU.mult, op1=ALU.subtract))
                        dve_do(V.tensor_scalar(far[:, :], far[:, :], float((NE - 1) * CAP), None, ALU.add))
                        dve_do(V.scalar_tensor_tensor(out=tmp[:, :, :], in0=rank[:, :, :], scalar=float(CAP),
                                                      in1=far[:, :].unsqueeze(1).to_broadcast([128, NT, NE]),
                                                      op0=ALU.is_ge, op1=ALU.mult))
                        dve_do(V.tensor_tensor(rank[:, :, :], rank[:, :, :], tmp[:, :, :], ALU.add))
                        dve_do(V.tensor_tensor(rank[:, :, :], rank[:, :, :], row("ecap", NE), ALU.add))
                        for k in range(2):
                            dve_do(V.tensor_tensor(tmp[:, :, :], rank[:, :, :], oh[:, k], ALU.mult))
                            dve_do(V.reduce_sum(st[:, 9 + k, :], tmp[:, :, :], AX_X))
                        dve_do(V.tensor_tensor(ovm[:, :, :], ovb[0:1, 1:NE + 1].unsqueeze(1).to_broadcast([1, NOVER, NE]),
                                               C("iota")[0:1, 0:NOVER].unsqueeze(2).to_broadcast([1, NOVER, NE]), ALU.is_le))
                        dve_do(V.reduce_sum(ovf[:, 0:NOVER], ovm[:, :, :], AX_X))
                        dve_do(V.tensor_scalar(ovf[:, 0:NOVER], ovf[:, 0:NOVER], float(NE - 1), None, ALU.min))
                        dve_do(V.tensor_copy(ovf[:, NOVER:NOVER + 1], ovb[0:1, NE:NE + 1]))
                        dve_do(V.tensor_copy(over_i[:, :], ovf[:, :]))
                        V.tensor_copy(pos_i[:, :, :], st[:, 9:11, :]).then_inc(s_pos, 1)
                        dve_do.done()

                    @block.gpsimd
                    def _(pool):
                        pool.wait_ge(s_pos, 1)
                        pool.wait_ge(s_zeroed, 16 * (2 * NSLOT // 128 - NE * CAP // 128))
                        for k in range(2):
                            for t, rows in TILES:
                                pool.indirect_dma_start(out=xs_rows, out_offset=bass.IndirectOffsetOnAxis(
                                    ap=pos_i[0:rows, k, t:t + 1], axis=0), in_=xn[0:rows, t, :], in_offset=None).then_inc(s_disp, 16)
                        pool.wait_ge(s_disp, 32 * NT)

            with ExitStack() as ph, nc.Block() as block:
                xs = [sb(f"xs{s}_" + L, [CAP, D], to=ph) for s in range(WSLOTS)]
                xsT = [sb(f"xsT{s}_" + L, [128, KT, CAP], to=ph) for s in range(2)]
                sg = sb("sg" + L, [128, 2, 2, CAP], to=ph)
                hT = sb("hT" + L, [128, 2, 2, CAP], to=ph)
                ysb = [sb(f"ysb{s}_" + L, [CAP, D], to=ph) for s in range(WSLOTS)]
                s_xt = [lsem(f"xs_turned{s}") for s in range(2)]
                s_xe = [lsem(f"xsT_ready{s}") for s in range(2)]
                s_gu = [lsem(f"gate_up_done{s}") for s in range(2)]
                s_si = [lsem(f"silu_ready{s}") for s in range(2)]
                s_h = [lsem(f"h_ready{s}") for s in range(2)]
                s_dn = [lsem(f"down_done{s}") for s in range(WSLOTS)]
                s_ye = [lsem(f"y_copied{s}") for s in range(2)]
                s_yo = [lsem(f"y_stored{s}") for s in range(WSLOTS)]
                o_in, o_xt, o_xe, o_gu, o_si, o_h, o_dn, o_ye, o_yo = (
                    lsem("over_" + n) for n in ("in", "turned", "xsT", "gate_up", "silu", "h", "down", "copied", "stored"))
                s_end = lsem("over_all_stored")
                ROUNDS = NE // WSLOTS

                def load(eng, s, e, row0, sig):
                    load_weights(eng, s, e, sig)
                    load_rows(eng, s, row0, sig)

                def turn_rows(pe, s, q, sig, product=False):
                    for k in range(KT):
                        out, rows = bank(2)[:, CAP * k:CAP * k + CAP], xs[s][:, k:D:KT]
                        if product:
                            last = nc.tensor.matmul(out, rows, ident[0:CAP, 0:CAP], start=True, stop=True)
                        else:
                            last = nc.tensor.transpose(out, rows, ident[0:CAP, 0:CAP])
                    last.then_inc(sig, 1)

                def gate_up(pe, s, q, f, sig):
                    for j, wt in enumerate((wg[s], wu[s])):
                        for k in range(KT):
                            last = nc.tensor.matmul(bank(f)[:, CAP * j:CAP * j + CAP], wt[:, k, f:FE:2],
                                                    xsT[q][:, k, :], start=(k == 0), stop=(k == KT - 1))
                    last.then_inc(sig, 1)

                def down(pe, s, q, f):
                    for n in range(2):
                        last = nc.tensor.matmul(bank(4 + 2 * q + n)[0:CAP, :], hT[:, q, f, :], wd[s][:, f, 512 * n:512 * n + 512],
                                                start=(f == 0), stop=(f == 1))
                    return last

                def silu(q, f):
                    return nc.scalar.activation(sg[:, q, f, :], bank(f)[:, 0:CAP], ACT.Silu)

                def mul_up(q, f):
                    return nc.vector.tensor_tensor(hT[:, q, f, :], sg[:, q, f, :], bank(f)[:, CAP:2 * CAP], ALU.mult)

                @contextmanager
                def further_blocks(eng):
                    count = eng.value_load(over_i[0:1, NOVER:NOVER + 1], min_val=0, max_val=NOVER)
                    with eng.If(count > 0):
                        with eng.Fori(0, count) as m:
                            yield m, count
                        if eng is nc.vector:
                            eng.wait_ge(o_yo, 16 * count + 1)
                            nc.vector.memset(sg[:, 0, 0, 0:1], 0.0).then_inc(s_end, 1)
                            eng.wait_ge(s_end, 1)

                @block.sync
                def _(sp):
                    open_ring(sp, s_xe + s_h + s_ye + s_yo + [o_dn, o_ye, o_yo])
                    for s in range(WSLOTS):
                        load_rows(sp, s, s * CAP, s_in[s])

                    def store(s, i):
                        row = (i * WSLOTS + s) * CAP
                        if not isinstance(row, int):
                            row = sp.snap(row)
                        sp.wait_ge(s_ye[s % 2], 4 * i + 2 * (s // 2) + 3)
                        sp.dma_start(ys_rows[ds(row, CAP), :], ysb[s][:, :]).then_inc(s_yo[s], 16)

                    with sp.Fori(0, ROUNDS - 1) as i:
                        for s in range(WSLOTS):
                            sp.wait_ge(s_dn[s], i + 1)
                            load(sp, s, (i + 1) * WSLOTS + s, ((i + 1) * WSLOTS + s) * CAP, s_in[s])
                            store(s, i)
                    for s in range(WSLOTS):
                        store(s, ROUNDS - 1)
                    for s in range(WSLOTS):
                        sp.wait_ge(s_yo[s], 16 * ROUNDS + 1)
                    with further_blocks(sp) as (m, _):
                        e = sp.value_load(over_i[0:1, ds(m, 1)], min_val=0, max_val=NE - 1)
                        row = sp.snap((m + NE) * CAP)
                        sp.wait_ge(o_dn, m + 1)
                        load(sp, 0, e, row, o_in)
                        sp.wait_ge(o_ye, 2 * m + 3)
                        sp.dma_start(ys_rows[ds(row, CAP), :], ysb[0][:, :]).then_inc(o_yo, 16)

                @block.tensor
                def _(pe):
                    pe.wait_ge(s_in[0], 64)
                    turn_rows(pe, 0, 0, s_xt[0])

                    def body(i, last_round):
                        for s in range(WSLOTS):
                            q, r = s % 2, s // 2
                            pe.wait_ge(s_xe[q], 2 * i + r + 2)
                            gate_up(pe, s, q, 0, s_gu[q])
                            s1, q1 = (s + 1) % WSLOTS, 1 - q
                            more = not (last_round and s == WSLOTS - 1)
                            if more:
                                pe.wait_ge(s_in[s1], 64 * (i + 1 + (s == WSLOTS - 1)))
                            gate_up(pe, s, q, 1, s_gu[q])
                            if more:
                                turn_rows(pe, s1, q1, s_xt[q1])
                            pe.wait_ge(s_ye[q], 4 * i + 2 * r + 1)
                            for f in range(2):
                                pe.wait_ge(s_h[q], 4 * i + 2 * r + f + 2)
                                last = down(pe, s, q, f)
                            last.then_inc(s_dn[s], 1)

                    with pe.Fori(0, ROUNDS - 1) as i:
                        body(i, False)
                    body(ROUNDS - 1, True)
                    with further_blocks(pe) as (m, _):
                        pe.wait_ge(o_in, 64 * m + 64)
                        turn_rows(pe, 0, 0, o_xt, product=True)
                        pe.wait_ge(o_xe, m + 1)
                        for f in range(2):
                            gate_up(pe, 0, 0, f, o_gu)
                        pe.wait_ge(o_h, 2 * m + 2)
                        pe.wait_ge(o_ye, 2 * m + 1)
                        down(pe, 0, 0, 0)
                        down(pe, 0, 0, 1).then_inc(o_dn, 1)

                @block.scalar
                def _(act):
                    def xt_copy(q, value):
                        act.wait_ge(s_xt[q], value)
                        nc.scalar.activation(xsT[q][:, :, :].rearrange("p k c -> p (k c)"), bank(2)[:, 0:KT * CAP], ACT.Copy).then_inc(s_xe[q], 1)

                    xt_copy(0, 1)

                    def body(i, last_round):
                        for s in range(WSLOTS):
                            q, r = s % 2, s // 2
                            for f in range(2):
                                act.wait_ge(s_gu[q], 4 * i + 2 * r + f + 1)
                                act.wait_ge(s_h[q], 4 * i + 2 * r + 1)
                                silu(q, f).then_inc(s_si[q], 1)
                            if not (last_round and s == WSLOTS - 1):
                                q1 = 1 - q
                                xt_copy(q1, 2 * i + (s + 1) // 2 + 1)
                            act.wait_ge(s_dn[s], i + 1)
                            act.wait_ge(s_yo[s], 16 * i + 1)
                            nc.scalar.activation(ysb[s][:, 0:512], bank(4 + 2 * q)[0:CAP, :], ACT.Copy).then_inc(s_ye[q], 1)

                    with act.Fori(0, ROUNDS - 1) as i:
                        body(i, False)
                    body(ROUNDS - 1, True)
                    with further_blocks(act) as (m, _):
                        act.wait_ge(o_xt, m + 1)
                        nc.scalar.activation(xsT[0][:, :, :].rearrange("p k c -> p (k c)"), bank(2)[:, 0:KT * CAP], ACT.Copy).then_inc(o_xe, 1)
                        act.wait_ge(o_gu, 2 * m + 2)
                        silu(0, 0).then_inc(o_si, 1)
                        silu(0, 1).then_inc(o_si, 1)
                        act.wait_ge(o_dn, m + 2)
                        act.wait_ge(o_yo, 16 * m + 1)
                        nc.scalar.activation(ysb[0][:, 0:512], bank(4)[0:CAP, :], ACT.Copy).then_inc(o_ye, 1)

                @block.vector
                def _(dve):
                    def body(i):
                        for s in range(WSLOTS):
                            q, r = s % 2, s // 2
                            for f in range(2):
                                dve.wait_ge(s_si[q], 4 * i + 2 * r + f + 1)
                                dve.wait_ge(s_gu[q], 4 * i + 2 * r + f + 1)
                                mul_up(q, f).then_inc(s_h[q], 1)
                            dve.wait_ge(s_dn[s], i + 1)
                            dve.wait_ge(s_yo[s], 16 * i + 1)
                            nc.vector.tensor_copy(ysb[s][:, 512:D], bank(5 + 2 * q)[0:CAP, :]).then_inc(s_ye[q], 1)

                    with dve.Fori(0, ROUNDS) as i:
                        body(i)
                    with further_blocks(dve) as (m, _):
                        dve.wait_ge(o_si, 2 * m + 2)
                        mul_up(0, 0).then_inc(o_h, 1)
                        mul_up(0, 1).then_inc(o_h, 1)
                        dve.wait_ge(o_dn, m + 2)
                        dve.wait_ge(o_yo, 16 * m + 1)
                        nc.vector.tensor_copy(ysb[0][:, 512:D], bank(5)[0:CAP, :]).then_inc(o_ye, 1)

            with ExitStack() as ph, nc.Block() as block:
                yr = sb("yr" + L, [128, 2 * NT, D], to=ph)
                s_gt, s_cb = [lsem(f"y_back{k}") for k in range(2 * NT)], lsem("y_added")

                @block.gpsimd
                def _(pool):
                    for t, rows in TILES:
                        for k in range(2):
                            pool.indirect_dma_start(out=yr[0:rows, 2 * t + k, :], out_offset=None, in_=ys_rows,
                                                    in_offset=bass.IndirectOffsetOnAxis(ap=pos_i[0:rows, k, t:t + 1], axis=0)
                                                    ).then_inc(s_gt[2 * t + k], 16)

                @block.vector
                def _(dve):
                    n = 0
                    for t, rows in TILES:
                        for k in range(2):
                            dve.wait_ge(s_gt[2 * t + k], 16)
                            nc.vector.scalar_tensor_tensor(out=x[0:rows, t, :], in0=yr[0:rows, 2 * t + k, :],
                                                           scalar=wts[0:rows, k, t:t + 1], in1=x[0:rows, t, :],
                                                           op0=ALU.mult, op1=ALU.add).then_inc(s_cb, 1)
                            n += 1
                            dve.wait_ge(s_cb, n)

        @scoped
        def layer_b():
            phB = ExitStack()
            xkT = sb("xkT_b", [128, KT, TOK], to=phB)
            xqT = sb("xqT_b", [128, KT, TOK], to=phB)
            norm_phase([a["g_kv"], a["g_attn"][1]], [xkT, xqT])
            w_kv = a["w_kv_b"].rearrange("(p t) n -> p t n", t=KT)
            w_q = a["w_q_b"][0].rearrange("(p t) n -> p t n", t=KT)
            UW = HD + KQ

            with phB, ExitStack() as ph, nc.Block() as block:
                wB = sb("wB", [128, NDIL, KT, UW], to=ph)
                pT = sb("pT", [128, 3, TOK], to=ph)
                tok = sb("tok", [128, NDIL, NT, UW], to=ph)
                kk = sb("kk", [128, 4, 2 * HD], to=ph)
                kT = sb("kT", [128, SEQ], to=ph)
                qT = sb("qT", [128, 2, SEQ], to=ph)
                vp = sb("vp", [128, 2, 4, HD], to=ph)
                sc = sb("sc", [128, 2, 4, 256], to=ph)
                pTs = sb("pTs", [128, 2, 8 * 128], to=ph)
                nm = sb("nm", [128, 2, 4], to=ph)
                junk = sb("junk_b", [128, 1], to=ph)
                ost = sb("ost", [128, NDIL, 4, 4, HD + 2], to=ph)
                cw = sb("cw", [128, 5, 4, 4], to=ph)
                ce = sb("ce", [128, NDIL, 4, 4], to=ph)
                oc = sb("oc", [128, 4, 4, HD], to=ph)
                ot = sb("ot", [128, 4, 4, HD], to=ph)
                sq = sb("sq", [128, NT, KQ], to=ph)
                rp = sb("rp", [128, 4, NT, 5, 8], to=ph)
                gn = sb("gn", [128, 2, NDIL, HD], to=ph)
                gain = sb("gain", [128, NDIL, KQ], to=ph)
                s_w = [sem(f"wb{g}_in") for g in range(NDIL)]
                s_kvo = [sem(f"b_kv_stored{g}") for g in range(NDIL)]
                (s_gn, s_gain, s_proj, s_pev, s_tt, s_tk, s_vc, s_rope, s_tb, s_tbc, s_qk, s_sev, s_mx, s_ex, s_tp,
                 s_ptc, s_pv, s_oc, s_od, s_ob, s_cm, s_ce, s_comb, s_to, s_toc, s_kk) = (
                    sem("b_" + n) for n in (
                        "gains_in", "gain_ready", "proj_done", "proj_copied", "tok_turned", "tok_copied", "v_turn_copied",
                        "rope_done", "qk_turned", "qk_copied", "scores_done", "scores_read", "max_ready",
                        "exp_ready", "p_turned", "p_copied", "pv_done", "o_copied", "o_out", "o_back", "max_diff",
                        "max_exp", "combined", "o_turned", "oT_ready", "k_doubled"))

                def kv_cols(j, g, part):
                    return ds(g * 512 + part * 256 + j * HD, HD)

                WINDOW = (1, 2, 0)

                def two_on(j, k):
                    return (j, 2) if k == 0 else (j + 1, k - 1)

                @block.sync
                def _(sp):
                    for s in (s_tp, s_pv, s_oc):
                        sp.nop().then_inc(s, 1)
                        sp.nop().then_inc(s, 1)
                    for s in (s_sev, s_ptc):
                        sp.nop().then_inc(s, 1)
                    sp.dma_start(gn[:, 0], a["k_norm_b"].partition_broadcast(128)).then_inc(s_gn, 16)
                    sp.dma_start(gn[:, 1], a["q_norm_b"][0].partition_broadcast(128)).then_inc(s_gn, 16)

                    def load(j, g):
                        sp.dma_start(wB[:, g, :, 0:HD], w_kv[:, :, kv_cols(j, g, 1)]).then_inc(s_w[g], 16)
                        sp.dma_start(wB[:, g, :, HD:2 * HD], w_kv[:, :, kv_cols(j, g, 0)]).then_inc(s_w[g], 16)
                        sp.dma_start(wB[:, g, :, 2 * HD:], w_q[:, :, ds(g * D + j * 256, 256)]).then_inc(s_w[g], 16)

                    def next_weights(j, k):
                        sp.wait_ge(s_proj, 6 * (3 * j + k) + 6)
                        load(j + 1, WINDOW[k])

                    def store_kv(j, k):
                        g = WINDOW[k]
                        sp.wait_ge(s_rope, 3 * j + k + 1)
                        out_p, out_s, rows = kv_out[g]
                        t0 = (SEQ - rows) // 128
                        for part, c in ((1, 0), (0, HD)):
                            sp.dma_start(out_p[0, :, part, ds(j, 1), :].rearrange("(t p) a e -> p t (a e)", p=128),
                                         tok[:, g, t0:4, c:c + HD]).then_inc(s_kvo[g], 16)
                            sp.dma_start(out_s[:, 0, part, ds(j, 1), :].rearrange("b a e -> b (a e)"),
                                         tok[0:DEC, g, 4, c:c + HD]).then_inc(s_kvo[g], 16)
                        sp.dma_start(s_rows[g, :, ds(j, 1), :].rearrange("b a e -> b (a e)"), tok[0:DEC, g, 4, :]).then_inc(s_kvo[g], 16)

                    def reorder(j, k):
                        g = WINDOW[k]
                        sp.wait_ge(s_oc, 4 * (3 * j + k) + 4 + 2)
                        sp.dma_start(o_rows[g - 1].rearrange("(i r) x -> i (r x)", r=4),
                                     ost[:, g].rearrange("p r h e -> p (r h e)")).then_inc(s_od, 16)
                        sp.wait_ge(s_od, 16 * (2 * j + g))
                        sp.dma_start(ost[:, g].rearrange("p t h e -> p t (h e)"),
                                     o_rows[g - 1].rearrange("(t p) x -> p t x", p=128)).then_inc(s_ob, 16)

                    for g in WINDOW:
                        load(0, g)
                    for k in range(2):
                        next_weights(0, k)
                    store_kv(0, 0)

                    def body(j, left):
                        for k in range(NDIL):
                            if left >= (1 if k == 0 else 2):
                                next_weights(*two_on(j, k))
                            if left or k < 2:
                                store_kv(*((j, k + 1) if k < 2 else (j + 1, 0)))
                            if k < 2:
                                reorder(j, k)

                    with sp.Fori(0, NKV - 2) as j:
                        body(j, 2)
                    body(NKV - 2, 1)
                    body(NKV - 1, 0)
                    for g in range(NDIL):
                        sp.wait_ge(s_kvo[g], 80 * NKV)

                @block.tensor
                def _(pe):
                    def project(j, k, f, h):
                        n, g = 3 * j + k, WINDOW[k]
                        if f == 0:
                            if h == 0:
                                pe.wait_ge(s_w[g], 48 * j + 48)
                            if not (isinstance(n, int) and n == 0):
                                if h == 0:
                                    pe.wait_ge(s_tk, 5 * n)
                                else:
                                    pe.wait_ge(s_vc, n)
                        else:
                            pe.wait_ge(s_pev, 6 * n + 2 * (f - 1) + h + 1)
                        xT = xkT if f == 0 else xqT
                        for kt in range(KT):
                            last = nc.tensor.matmul(bank(h)[:, 0:HALF], wB[:, g, kt, 128 * f:128 * f + 128],
                                                    xT[:, kt, HALF * h:HALF * h + HALF], start=(kt == 0), stop=(kt == KT - 1))
                        last.then_inc(s_proj, 1)

                    def turn_tok(j, k, t):
                        n, rows = 3 * j + k, TILES[t][1]
                        if t < 2:
                            pe.wait_ge(s_pev, 6 * n + 6)
                        else:
                            pe.wait_ge(s_tk, 5 * n + (t - 1 if t < 4 else 4))
                        for f in range(3):
                            last = nc.tensor.transpose(bank(t % 2)[0:rows, 128 * f:128 * f + 128],
                                                       pT[:, f, 128 * t:128 * t + rows], ident)
                        last.then_inc(s_tt, 1)
                        if t == 4 and WINDOW[k]:
                            for r in range(4):
                                last = nc.tensor.transpose(bank(1)[:, HD * r:HD * r + HD], pT[0:HD, 0, r:SEQ:4], ident[0:HD, 0:HD])
                            last.then_inc(s_tt, 1)

                    def front(j, k):
                        for f in range(3):
                            for h in range(2):
                                project(j, k, f, h)
                        for t in range(NT):
                            turn_tok(j, k, t)

                    def weave(j, k, more, turned):
                        n, g = 3 * j + k, WINDOW[k]

                        def ahead(step, *at):
                            if more:
                                step(*two_on(j, k), *at)

                        def turn_back(f):
                            for t in range(4):
                                src = kk[:, t, :] if f == 2 else tok[:, g, t, 128 * f + 128:128 * f + 256]
                                last = nc.tensor.transpose(bank(6 + f % 2)[:, 128 * t:128 * t + 128], src, ident)
                            last.then_inc(s_tb, 1)

                        def qk(h):
                            rows = slice(64 * (h % 2), 64 * (h % 2) + 64)
                            pe.wait_ge(s_sev, 4 * n + h + 1)
                            q, k = qT[rows, h // 2, :], kT[rows, :]
                            for b in range(4):
                                if g == 0:
                                    o = ps[:, 2048 + 256 * b:2048 + 256 * b + 256]
                                    if b:
                                        last = nc.tensor.matmul(o, q[:, 128 * b:128 * b + 128], k[:, 128 * b - 128:128 * b + 128],
                                                                start=True, stop=True)
                                    else:
                                        for half in range(2):
                                            nc.tensor.matmul(o[:, 128 * half:128 * half + 128], q[:, 0:128], k[:, 0:128],
                                                             start=True, stop=True)
                                else:
                                    last = nc.tensor.matmul(bank(4)[:, 128 * b:128 * b + 128], q[:, b:SEQ:4], k[:, b:SEQ:4],
                                                            start=True, stop=True)
                            last.then_inc(s_qk, 1)

                        def turn_p(h):
                            pe.wait_ge(s_ex, 4 * n + h + 1)
                            pe.wait_ge(s_ptc, 4 * n + h + 1)
                            for b in range(4):
                                for half in range(2 if g == 0 else 1):
                                    o = 3072 + (256 * b + 128 * half if g == 0 else 128 * b)
                                    last = nc.tensor.transpose(ps[:, o:o + 128], sc[:, h % 2, b, 128 * half:128 * half + 128], ident)
                            last.then_inc(s_tp, 1)

                        def pv(h):
                            pe.wait_ge(s_ptc, 4 * n + h + 2)
                            pe.wait_ge(s_oc, 4 * n + h + 1)
                            for b in range(4):
                                o = bank(2 + h % 2)[:, HD * b:HD * b + HD]
                                if g == 0:
                                    for half in ((0, 1) if b else (1,)):
                                        c = 256 * b + 128 * half
                                        last = nc.tensor.matmul(o, pTs[:, h % 2, c:c + 128], tok[:, 0, b - 1 + half, 0:HD],
                                                                start=(half == 0 or b == 0), stop=(half == 1))
                                else:
                                    last = nc.tensor.matmul(o, pTs[:, h % 2, 128 * b:128 * b + 128], vp[:, g - 1, b, :],
                                                            start=True, stop=True)
                            last.then_inc(s_pv, 1)

                        pe.wait_ge(s_rope, n + 1)
                        pe.wait_ge(s_ptc, 4 * n + 1)
                        turn_back(0)
                        turn_back(1)
                        ahead(project, 0, 0)
                        pe.wait_ge(s_tbc, 3 * n + 1)
                        pe.wait_ge(s_kk, n + 1)
                        turn_back(2)
                        ahead(project, 0, 1)
                        pe.wait_ge(s_tbc, 3 * n + 3)
                        qk(0)
                        ahead(project, 1, 0)
                        if turned:
                            turn_o(j - 1)
                        qk(1)
                        if turned:
                            pe.wait_ge(s_toc, j)
                        turn_p(0)
                        ahead(project, 1, 1)
                        qk(2)
                        turn_p(1)
                        pv(0)
                        ahead(project, 2, 0)
                        qk(3)
                        turn_p(2)
                        pv(1)
                        ahead(project, 2, 1)
                        ahead(turn_tok, 0)
                        ahead(turn_tok, 1)
                        turn_p(3)
                        pv(2)
                        ahead(turn_tok, 2)
                        ahead(turn_tok, 3)
                        pv(3)
                        ahead(turn_tok, 4)

                    def turn_o(j):
                        pe.wait_ge(s_comb, j + 1)
                        for f in range(2):
                            for t in range(4):
                                last = nc.tensor.transpose(bank(6 + f)[:, 128 * t:128 * t + 128], flat(oc[:, t, 2 * f:2 * f + 2, :]), ident)
                        last.then_inc(s_to, 1)

                    front(0, 0)
                    front(0, 1)

                    def body(j, first, last):
                        for k in range(NDIL):
                            weave(j, k, not last or k == 0, k == 0 and not first)

                    body(0, True, False)
                    with pe.Fori(1, NKV - 1) as j:
                        body(j, False, False)
                    body(NKV - 1, False, True)
                    turn_o(NKV - 1)

                @block.scalar
                def _(act):
                    def proj_copy(j, k, f, h):
                        act.wait_ge(s_proj, 6 * (3 * j + k) + 2 * f + h + 1)
                        nc.scalar.activation(pT[:, f, HALF * h:HALF * h + HALF], bank(h)[:, 0:HALF], ACT.Copy).then_inc(s_pev, 1)

                    def front(j, k):
                        for f in range(3):
                            for h in range(2):
                                proj_copy(j, k, f, h)

                    def weave(j, k, more):
                        n, g = 3 * j + k, WINDOW[k]

                        def ahead(*at):
                            if more:
                                proj_copy(*two_on(j, k), *at)

                        def turned_copy(f):
                            act.wait_ge(s_tb, 3 * n + f + 1)
                            dst = kT[:, :] if f == 2 else qT[:, f, :]
                            nc.scalar.activation(dst, bank(6 + f % 2), ACT.Copy).then_inc(s_tbc, 1)

                        def exps(h):
                            act.wait_ge(s_mx, 4 * n + h + 1)
                            width = 256 if g == 0 else 128
                            for b in range(4):
                                last = nc.scalar.activation(sc[:, h % 2, b, 0:width], sc[:, h % 2, b, 0:width], ACT.Exp,
                                                            bias=nm[:, h % 2, b:b + 1], accum_out=ost[:, g, b, h, HD + 1:HD + 2])
                            last.then_inc(s_ex, 1)

                        def p_copy(h):
                            act.wait_ge(s_tp, 4 * n + h + 1 + 2)
                            act.wait_ge(s_pv, 4 * n + h + 1)
                            width = 1024 if g == 0 else 512
                            nc.scalar.activation(pTs[:, h % 2, 0:width], ps[:, 3072:3072 + width], ACT.Copy).then_inc(s_ptc, 1)

                        act.wait_ge(s_rope, n + 1)
                        nc.scalar.activation(kk[:, :, :].rearrange("p t (a e) -> p t a e", a=2),
                                             tok[:, g, 0:4, HD:2 * HD].unsqueeze(2).to_broadcast([128, 4, 2, HD]),
                                             ACT.Copy).then_inc(s_kk, 1)
                        turned_copy(0)
                        turned_copy(1)
                        ahead(0, 0)
                        turned_copy(2)
                        ahead(0, 1)
                        exps(0)
                        ahead(1, 0)
                        p_copy(0)
                        exps(1)
                        ahead(1, 1)
                        p_copy(1)
                        exps(2)
                        ahead(2, 0)
                        p_copy(2)
                        exps(3)
                        ahead(2, 1)
                        p_copy(3)

                    front(0, 0)
                    front(0, 1)

                    def body(j, last):
                        for k in range(NDIL):
                            weave(j, k, not last or k == 0)
                        act.wait_ge(s_cm, j + 1)
                        nc.scalar.activation(ce[:, :, :, :], ce[:, :, :, :], ACT.Exp).then_inc(s_ce, 1)

                    with act.Fori(0, NKV - 1) as j:
                        body(j, False)
                    body(NKV - 1, True)

                @block.vector
                def _(dve):
                    dve_do.on(dve)
                    V = nc.vector
                    dve_do(V.memset(tok[:, :, 4, :], 0.0))
                    dve.wait_ge(s_gn, 32)
                    dve_do(V.tensor_scalar(gain[:, :, 0:HD], gn[:, 0], HD ** 0.5, None, ALU.mult))
                    V.tensor_scalar(gain[:, :, HD:].rearrange("p g (h e) -> p g h e", h=4),
                                    gn[:, 1].unsqueeze(2).to_broadcast([128, NDIL, 4, HD]), HD ** 0.5, None, ALU.mult).then_inc(s_gain, 1)
                    dve_do.done()

                    def tok_copy(j, k, t):
                        n, g, rows = 3 * j + k, WINDOW[k], TILES[t][1]
                        if t == 0 and (not isinstance(j, int) or j):
                            dve.wait_ge(s_kvo[g], 80 * j)
                            dve.wait_ge(s_tb, 3 * (n - 2))
                            if g == 0:
                                dve.wait_ge(s_pv, 4 * (n - 2) + 2)
                        tt = 5 * n + 2 * j + k
                        dve.wait_ge(s_tt, tt + t + 1)
                        V.tensor_copy(tok[0:rows, g, t, :], bank(t % 2)[0:rows, 0:UW]).then_inc(s_tk, 1)
                        if t == 4:
                            if g:
                                dve.wait_ge(s_tt, tt + 6)
                                V.tensor_copy(flat(vp[:, g - 1]), bank(1)[:, 0:4 * HD]).then_inc(s_vc, 1)
                            else:
                                V.memset(junk[:, :], 0.0).then_inc(s_vc, 1)

                    def weave(j, k, more, turned):
                        n, g = 3 * j + k, WINDOW[k]

                        def ahead(t):
                            if more:
                                tok_copy(*two_on(j, k), t)

                        def soft(h):
                            dve.wait_ge(s_qk, 4 * n + h + 1)
                            dve.wait_ge(s_tp, 4 * n + h + 1)
                            if g == 0:
                                dst, src = sc[:, h % 2, :, :], ps[:, 2048:3072].rearrange("p (b k) -> p b k", b=4)
                                mask = C("m0").rearrange("p (b k) -> p b k", b=4)
                            else:
                                dst, src = sc[:, h % 2, :, 0:128], bank(4).rearrange("p (b k) -> p b k", b=4)
                                mask = C(f"m{g}").unsqueeze(1).to_broadcast([128, 4, 128])
                            V.scalar_tensor_tensor(out=dst, in0=src, scalar=SCALE, in1=mask, op0=ALU.mult, op1=ALU.add).then_inc(s_sev, 1)
                            dve.wait_ge(s_sev, 4 * n + h + 2)
                            top = ost[:, g, :, h, HD:HD + 1].rearrange("p b a -> p (b a)")
                            dve_do(V.tensor_reduce(top, dst, AX_X, ALU.max))
                            V.tensor_scalar(nm[:, h % 2, :], top, -1.0, None, ALU.mult).then_inc(s_mx, 1)

                        def o_copy(h):
                            dve.wait_ge(s_pv, 4 * n + h + 1 + 2)
                            V.tensor_copy(ost[:, g, :, h, 0:HD], bank(2 + h % 2)[:, 0:4 * HD].rearrange("p (b e) -> p b e", b=4)).then_inc(s_oc, 1)

                        soft(0)
                        if turned:
                            turn_copy(j - 1)
                        soft(1)
                        soft(2)
                        o_copy(0)
                        soft(3)
                        o_copy(1)
                        ahead(0)
                        ahead(1)
                        o_copy(2)
                        ahead(2)
                        ahead(3)
                        o_copy(3)
                        ahead(4)

                    def combine(j):
                        dve.wait_ge(s_ob, 32 * j + 32)

                        def mx(g):
                            return ost[:, g, :, :, HD:HD + 1].rearrange("p t h a -> p t (h a)")

                        def sm(g):
                            return ost[:, g, :, :, HD + 1:HD + 2].rearrange("p t h a -> p t (h a)")

                        dve.wait_ge(s_oc, 12 * j + 14)
                        dve_do(V.tensor_tensor(cw[:, 0], mx(0), mx(1), ALU.max))
                        dve_do(V.tensor_tensor(cw[:, 0], cw[:, 0], mx(2), ALU.max))
                        for g in range(NDIL):
                            ins = V.tensor_tensor(ce[:, g], mx(g), cw[:, 0], ALU.subtract)
                            if g < 2:
                                dve_do(ins)
                        ins.then_inc(s_cm, 1)
                        dve.wait_ge(s_ce, j + 1)
                        for g in range(NDIL):
                            dve_do(V.tensor_tensor(cw[:, 1 + g], ce[:, g], sm(g), ALU.mult))
                        dve_do(V.tensor_tensor(cw[:, 1], cw[:, 1], cw[:, 2], ALU.add))
                        dve_do(V.tensor_tensor(cw[:, 1], cw[:, 1], cw[:, 3], ALU.add))
                        dve_do(V.reciprocal(cw[:, 4], cw[:, 1]))
                        for g in range(NDIL):
                            dve_do(V.tensor_tensor(ce[:, g], ce[:, g], cw[:, 4], ALU.mult))
                        for g in range(NDIL):
                            dve_do(V.tensor_tensor((ot if g else oc)[:, :, :, :], ost[:, g, :, :, 0:HD],
                                                   ce[:, g].unsqueeze(3).to_broadcast([128, 4, 4, HD]), ALU.mult))
                            if g:
                                ins = V.tensor_tensor(oc[:, :, :, :], oc[:, :, :, :], ot[:, :, :, :], ALU.add)
                                if g < 2:
                                    dve_do(ins)
                        ins.then_inc(s_comb, 1)

                    def turn_copy(j):
                        dve.wait_ge(s_to, j + 1)
                        V.tensor_copy(oT[:, ds(2 * j, 2), 0:SEQ], bank(6, 2).rearrange("p (f m) -> p f m", f=2)).then_inc(s_toc, 1)

                    for k in range(2):
                        for t in range(NT):
                            tok_copy(0, k, t)

                    def body(j, first, last):
                        for k in range(NDIL):
                            weave(j, k, not last or k == 0, k == 0 and not first)
                        combine(j)

                    per = 3 * 4 + 2 + 2 + 3 + 2 + 1 + 3 + 3 + 1
                    dve_do.enter(0, per)
                    body(0, True, False)
                    dve_do.leave(1)
                    with dve.Fori(1, NKV - 1) as j:
                        dve_do.enter(j - 1, per)
                        body(j, False, False)
                    dve_do.leave(NKV - 2)
                    dve_do.enter(0, per)
                    body(NKV - 1, False, True)
                    dve_do.leave(1)
                    turn_copy(NKV - 1)

                @block.gpsimd
                def _(pool):
                    pool_do.on(pool)
                    P = nc.gpsimd
                    pool.wait_ge(s_gain, 1)

                    def front(j, k):
                        n, g = 3 * j + k, WINDOW[k]
                        pool.wait_ge(s_tk, 5 * n + 5)
                        kq = tok[:, g, :, HD:]
                        s4 = sq[:, :, :].rearrange("p t (h e) -> p t h e", h=5)
                        pool_do(P.tensor_tensor(sq[:, :, :], kq, kq, ALU.mult))
                        w = HD // 2
                        while w:
                            pool_do(P.tensor_tensor(s4[:, :, :, 0:w], s4[:, :, :, 0:w], s4[:, :, :, w:2 * w], ALU.add))
                            w //= 2
                        ss = s4[:, :, :, 0]
                        shape = [128, NT, 5]
                        pool_do(P.tensor_tensor(ss, ss, C("eps64").unsqueeze(2).to_broadcast(shape), ALU.add))
                        pool_do(P.tensor_tensor(ss, ss, C("mhalf").unsqueeze(2).to_broadcast(shape), ALU.pow))
                        k4 = kq.rearrange("p t (h e) -> p t h e", h=5)
                        pool_do(P.tensor_tensor(k4, k4, s4[:, :, :, 0:1].to_broadcast([128, NT, 5, HD]), ALU.mult))
                        pool_do(P.tensor_tensor(kq, kq, gain[:, g, :].unsqueeze(1).to_broadcast([128, NT, KQ]), ALU.mult))
                        x1, x2 = k4[:, :, :, 0:8], k4[:, :, :, 8:16]
                        cos, sin = (C(m).rearrange("p (t e) -> p t e", e=8).unsqueeze(2).to_broadcast([128, NT, 5, 8])
                                    for m in ("cos", "sin"))
                        pool_do(P.tensor_tensor(rp[:, 0], x1, cos, ALU.mult))
                        pool_do(P.tensor_tensor(rp[:, 1], x2, sin, ALU.mult))
                        pool_do(P.tensor_tensor(rp[:, 2], x2, cos, ALU.mult))
                        pool_do(P.tensor_tensor(rp[:, 3], x1, sin, ALU.mult))
                        pool_do(P.tensor_tensor(x1, rp[:, 0], rp[:, 1], ALU.subtract))
                        P.tensor_tensor(x2, rp[:, 2], rp[:, 3], ALU.add).then_inc(s_rope, 1)

                    per = 3 * 16
                    with pool.Fori(0, NKV) as j:
                        pool_do.enter(j, per)
                        for k in range(NDIL):
                            front(j, k)
                    pool_do.leave(NKV)

            n1, n2 = PAST // 4 + 1, PAST // 16 + 1
            with ExitStack() as ph, nc.Block() as block:
                kb = sb("kb", [128, DEC, 2, 512], to=ph)
                sel = sb("sel", [NDIL * DEC, DEC * S1ROWS], to=ph)
                qs = sb("qs", [NDIL * DEC, D], to=ph)
                oh_b = sb("oh_b", [128, 2, NKV * HD], to=ph)
                out_b = OutProjection("b", a["w_o_b"][0], ph)
                s_oh0, s_ohc, s_ot = (sem("bs_" + n) for n in ("heads_zeroed", "heads_copied", "heads_turned"))
                prod = sb("prodb", [128, D], to=ph)
                SS = sb("SS", [128, 2, DEC, NH], to=ph)
                pr = sb("pr", [128, 256], to=ph)
                pt = sb("ptb", [128, 2, 128], to=ph)
                sml = sb("sml", [128, 4], to=ph)
                s_kb = [sem(f"bs_keys_in{b}") for b in range(DEC)]
                s_q, s_qb, s_e, s_z, s_st, s_mm, s_xx, s_pn, s_pt, s_pc, s_pv, s_fin = (
                    sem("bs_" + n) for n in ("q_in", "q_spread", "prod_done", "scores", "turned", "max", "exp", "normed",
                                             "p_turned", "p_copied", "pv_done", "o_ready"))
                srow = [s_rows[g].rearrange("b j e -> b (j e)") for g in range(NDIL)]

                @block.sync
                def _(sp):
                    sp.dma_start(sel[:, :], a["select"]).then_inc(s_q, 16)
                    for g in range(NDIL):
                        for j in range(NKV):
                            sp.dma_start(qs[DEC * g:DEC * g + DEC, 256 * j:256 * j + 256], s_rows[g, :, j, 2 * HD:]).then_inc(s_q, 16)
                    for b in range(DEC):
                        if b == 1:
                            out_b.load(sp)
                        sp.dma_start(kb[:, b, 0, :], a["cache_kv_b1"][b].rearrange("s c h e -> s (c h e)")).then_inc(s_kb[b], 16)
                        sp.dma_start(kb[0:n1 - 1, b, 1, :], a["cache_kv_b2"][b, 0:PAST:4].rearrange("s c h e -> s (c h e)")).then_inc(s_kb[b], 16)
                        sp.dma_start(kb[n1:n1 + n2 - 1, b, 1, :], a["cache_kv_b3"][b, 0:PAST:16].rearrange("s c h e -> s (c h e)")).then_inc(s_kb[b], 16)
                        for g, row in ((1, n1 - 1), (2, n1 + n2 - 1), (0, n1 + n2)):
                            for part, c in ((1, 0), (0, HD)):
                                sp.dma_start(kb[row:row + 1, b, 1, 256 * part:256 * part + 256].rearrange("p (j e) -> p j e", j=NKV),
                                             s_rows[g, b:b + 1, :, c:c + HD]).then_inc(s_kb[b], 16)

                @block.tensor
                def _(pe):
                    pe.wait_ge(s_q, 16 * (1 + NDIL * NKV))
                    for u in range(2 * DEC):
                        b, tile = u // 2, u % 2
                        if u >= 2:
                            pe.wait_ge(s_e, u - 1)
                        for n in range(2):
                            o = bank(2 * (u % 2) + n)
                            half = slice(512 * n, 512 * n + 512)
                            if tile == 0:
                                last = nc.tensor.matmul(o, ident[0:DEC, b:b + 1].to_broadcast([DEC, 128]), qs[0:DEC, half],
                                                        start=True, stop=True)
                            else:
                                last = nc.tensor.matmul(o[0:S1ROWS, :], sel[:, b * S1ROWS:b * S1ROWS + S1ROWS], qs[:, half],
                                                        start=True, stop=True)
                        last.then_inc(s_qb, 1)
                        if u % 2 and b:
                            out_b.product(pe, b - 1)
                    out_b.product(pe, DEC - 1)
                    pe.wait_ge(s_z, 2 * DEC + 1)
                    for tile in range(2):
                        last = nc.tensor.transpose(bank(4)[:, 128 * tile:128 * tile + 128], SS[:, tile].rearrange("p b h -> p (b h)"), ident)
                    last.then_inc(s_st, 1)
                    pe.wait_ge(s_pn, 1)
                    for tile in range(2):
                        last = nc.tensor.transpose(bank(5)[:, 128 * tile:128 * tile + 128], pr[:, 128 * tile:128 * tile + 128], ident)
                    last.then_inc(s_pt, 1)
                    pe.wait_ge(s_pc, 1)
                    for b in range(DEC):
                        for tile, rows in ((0, 128), (1, S1ROWS)):
                            last = nc.tensor.matmul(bank(b // 4)[32 * (b % 4):32 * (b % 4) + NH, 0:NKV * HD],
                                                    pt[0:rows, tile, NH * b:NH * b + NH], kb[0:rows, b, tile, 256:512],
                                                    start=(tile == 0), stop=(tile == 1))
                        if b % 4 == 3:
                            last.then_inc(s_pv, 1)
                    own = ident.rearrange("p (i h) -> p i h", i=4)
                    for q in range(2):
                        pe.wait_ge(s_ohc, 4 * q + 4)
                        for j in range(NKV):
                            for i in range(2):
                                o = 32 * q + 8 * j
                                last = nc.tensor.matmul(bank(4)[64 * i:64 * i + 64, o:o + 8], oh_b[:, q, HD * j:HD * j + HD],
                                                        own[:, :, 4 * j + i:4 * j + i + 3:2], start=True, stop=True)
                    last.then_inc(s_ot, 1)
                    pe.wait_ge(s_fin, 2)
                    for i in (8, 9):
                        out_b.product(pe, i)

                @block.vector
                def _(dve):
                    dve_do.on(dve)
                    V = nc.vector
                    V.memset(flat(oh_b), 0.0).then_inc(s_oh0, 1)
                    V.memset(SS[:, 1, :, :], NEG).then_inc(s_z, 1)
                    dve.wait_ge(s_z, 1)
                    for u in range(2 * DEC):
                        b, tile = u // 2, u % 2
                        rows = 128 if tile == 0 else S1ROWS
                        dve.wait_ge(s_qb, u + 1)
                        if tile == 0:
                            dve.wait_ge(s_kb[b], 16 * 9)
                        shape = [rows, NKV, 4, HD]
                        V.tensor_tensor(prod[0:rows, :].rearrange("p (j i e) -> p j i e", j=NKV, i=4),
                                        kb[0:rows, b, tile, 0:256].rearrange("p (j e) -> p j e", j=NKV).unsqueeze(2).to_broadcast(shape),
                                        bank(2 * (u % 2), 2)[0:rows, :].rearrange("p (j i e) -> p j i e", j=NKV, i=4), ALU.mult).then_inc(s_e, 1)
                        dve.wait_ge(s_e, u + 1)
                        V.reduce_sum(SS[0:rows, tile, b, :], prod[0:rows, :].rearrange("p (h e) -> p h e", e=HD), AX_X).then_inc(s_z, 1)
                        dve.wait_ge(s_z, u + 2)
                        if tile and b:
                            out_b.add(dve, b - 1)
                    out_b.add(dve, DEC - 1)
                    dve.wait_ge(s_st, 1)
                    dve_do(V.tensor_scalar(pr[:, :], bank(4)[:, 0:256], SCALE, None, ALU.mult))
                    dve_do(V.tensor_reduce(sml[:, 0:1], pr[:, :], AX_X, ALU.max))
                    V.tensor_scalar(sml[:, 1:2], sml[:, 0:1], -1.0, None, ALU.mult).then_inc(s_mm, 1)
                    dve.wait_ge(s_xx, 1)
                    dve_do(V.reciprocal(sml[:, 3:4], sml[:, 2:3]))
                    V.tensor_scalar(pr[:, :], pr[:, :], sml[:, 3:4], None, ALU.mult).then_inc(s_pn, 1)
                    dve.wait_ge(s_pt, 1)
                    V.tensor_copy(pt[:, :, :].rearrange("p a b -> p (a b)"), bank(5)[:, 0:256]).then_inc(s_pc, 1)
                    dve.wait_ge(s_oh0, 1)
                    for q in range(2):
                        dve.wait_ge(s_pv, q + 1)
                        for i in range(4):
                            rows = slice(32 * i, 32 * i + NH)
                            V.tensor_copy(oh_b[rows, q, :], bank(q)[rows, 0:NKV * HD]).then_inc(s_ohc, 1)
                    dve.wait_ge(s_ot, 1)
                    for q in range(2):
                        V.tensor_copy(oT[:, :, SEQ + 4 * q:SEQ + 4 * q + 4].rearrange("p (j m) i -> p j m i", m=2),
                                      bank(4)[:, 32 * q:32 * q + 32].rearrange("p (j i m) -> p j m i", j=NKV, i=4)).then_inc(s_fin, 1)
                    for i in (8, 9):
                        out_b.add(dve, i)
                    dve_do.done()

                @block.scalar
                def _(act):
                    act.wait_ge(s_mm, 1)
                    nc.scalar.activation(pr[:, :], pr[:, :], ACT.Exp, bias=sml[:, 1:2], accum_out=sml[:, 2:3]).then_inc(s_xx, 1)

        if stop != "A":
            with ExitStack() as phM:
                moe(0)
        if stop is None:
            layer_b()
            with ExitStack() as phM:
                moe(1)

        s_out = sem("y_stored")
        with nc.Block() as block:
            @block.sync
            def _(sp):
                sp.dma_start(y_prompt[0].rearrange("(t p) d -> p t d", p=128), x[:, 0:4, :]).then_inc(s_out, 16)
                sp.dma_start(y_sample[:, 0, :], x[0:DEC, 4, :]).then_inc(s_out, 16)
                sp.wait_ge(s_out, 32)


_INS = ["x_prompt", "x_sample", "cache_kv_a", "cache_kv_b1", "cache_kv_b2", "cache_kv_b3", "page_table", "g_attn", "g_ffn",
        "w_qkv_a", "w_o_a", "sb_bias", "g_kv", "w_kv_b", "k_norm_b", "w_q_b", "q_norm_b", "w_o_b", "w_router_group",
        "b_router_group", "w_router_expert", "b_router_expert", "w_gate", "w_up", "w_down"]
_OUTS = [(1, SEQ, D), (DEC, 1, D), (1, 1, SEQ, 2, NH, HD), (1, DEC, 1, 2, NH, HD),
         (1, 128, 2, NKV, HD), (DEC, 1, 2, NKV, HD), (1, SEQ, 2, NKV, HD), (DEC, 1, 2, NKV, HD),
         (1, SEQ, 2, NKV, HD), (DEC, 1, 2, NKV, HD)]


STOP = None


def kernel(**inputs):
    import numpy as _np
    import concourse.bacc as _bacc
    from concourse import mybir as _mybir
    from concourse.bass_utils import run_bass_kernel_spmd as _run

    nc = _bacc.Bacc("TRN2", target_bir_lowering=False, num_devices=1)
    arrays, aps = {}, {}
    given = {name: _np.ascontiguousarray(inputs[name]) for name in _INS}
    given["const"], given["select"] = constants(), selectors()
    for name, arr in given.items():
        arrays[f"in_{name}"] = arr
        aps[name] = nc.dram_tensor(f"in_{name}", arr.shape, _mybir.dt.from_np(arr.dtype), kind="ExternalInput").ap()
    outs = [nc.dram_tensor(f"out_{i}", shape, _mybir.dt.float32, kind="ExternalOutput").ap() for i, shape in enumerate(_OUTS)]
    build(nc, aps, outs, STOP)
    r = _run(nc, [arrays], core_ids=[0])
    return tuple(r.results[0][f"out_{i}"] for i in range(len(_OUTS)))
```

```python
from contextlib import ExitStack, contextmanager

import numpy as np

import concourse.bass as bass
from concourse import mybir

F32 = mybir.dt.float32
I32 = mybir.dt.int32
ALU = mybir.AluOpType
ACT = mybir.ActivationFunctionType
AX_X = mybir.AxisListType.X
ds = bass.ds

D = 1024
SEQ, DEC = 512, 8
TOK = SEQ + DEC
HALF = TOK // 2
TILES = [(t, 128) for t in range(SEQ // 128)] + [(SEQ // 128, DEC)]
NT = len(TILES)
KT = D // 128
HD = 64
NH = D // HD
NPAIR = NH // 2
PAST, PAGE = 256, 128
NCH = PAST // PAGE
SCALE = HD ** -0.5
EPS = 1e-6
NEG = -1e30
NKV = NH // 4
NDIL = 3
KQ = 5 * HD
NG, NE, EPG = 4, 32, 8
FE = D // 4
CAP = 64
NOVER = 2 * TOK // CAP
NSLOT = (NE + NOVER) * CAP
QSLOTS = 3
WSLOTS = 4

CONST = {}
_at = 0
for _name, _width in (("ident", 128), ("tri", 128), ("strict", 128), ("ones", 128),
                      ("cos", NT * 8), ("sin", NT * 8), ("valid", NT), ("iota", NE), ("iota99", NE),
                      ("ecap", NE), ("m0", 4 * 256), ("m1", 128), ("m2", 128), ("m3", 128), ("pidx", 1), ("eps", 1), ("eps64", NT), ("mhalf", NT)):
    CONST[_name] = (_at, _at + _width)
    _at += _width
NCONST = _at
S1ROWS = PAST // 4 + 1 + PAST // 16 + 1 + 1


def constants():
    c = np.zeros((128, NCONST), np.float32)

    def put(name, a):
        lo, hi = CONST[name]
        c[:, lo:hi] = np.asarray(a, np.float32).reshape(128, -1)

    p = np.arange(128)[:, None]
    m = np.arange(128)[None, :]
    put("ident", p == m)
    put("tri", p >= m)
    put("strict", p < m)
    put("ones", np.ones((128, 128)))
    pos = np.stack([np.arange(128) + 128 * t for t in range(NT)], 1).astype(np.float32)
    pos[:, NT - 1] = PAST
    half = HD // 8
    inv = np.power(np.float32(500000.0), -np.arange(half, dtype=np.float32) * np.float32(2.0) / np.float32(HD // 4))
    ang = (pos[:, :, None] * inv[None, None, :].astype(np.float32)).astype(np.float32)
    put("cos", np.cos(ang))
    put("sin", np.sin(ang))
    put("valid", np.stack([np.arange(128) < rows for _, rows in TILES], 1))
    put("iota", np.broadcast_to(np.arange(NE), (128, NE)))
    put("iota99", np.broadcast_to(np.arange(NE) + 99, (128, NE)))
    put("ecap", np.broadcast_to(np.arange(NE) * CAP, (128, NE)))
    m0 = np.full((128, 4, 256), NEG, np.float32)
    for b in range(4):
        if b:
            m0[:, b, 0:128] = np.where(m >= p, 0, NEG)
        m0[:, b, 128:256] = np.where(m <= p, 0, NEG)
    put("m0", m0)
    put("m1", np.where(m <= p, 0, NEG))
    put("m2", np.where((m <= p) & ((p - m) % 4 == 0), 0, NEG))
    put("m3", np.where(m > p, 0, NEG))
    put("pidx", 2 * np.arange(128))
    put("eps", np.full(128, EPS))
    put("eps64", np.full((128, NT), HD * EPS))
    put("mhalf", np.full((128, NT), -0.5))
    return c


class Steps:

    def __init__(self, sem):
        self.sem, self.total, self.n, self.base = sem, 0, 0, 0

    def on(self, eng):
        self.eng = eng

    def enter(self, i, per):
        self.base, self.n, self.per = self.total + i * per, 0, per

    def leave(self, count):
        assert self.n == self.per, (self.sem, self.n, self.per)
        self.total += count * self.per
        self.base, self.n = self.total, 0

    def done(self):
        self.total = self.base + self.n
        self.base, self.n = self.total, 0

    def __call__(self, ins):
        ins.then_inc(self.sem, 1)
        self.n += 1
        self.eng.wait_ge(self.sem, self.base + self.n)


def flat(ap):
    return ap.rearrange("p a b -> p (a b)")


def build(nc, a, outs):
    (y_prompt, y_sample, a_prompt, a_sample, b1p, b1s, b2p, b2s, b3p, b3s) = outs
    kv_out = ((b1p, b1s, 128), (b2p, b2s, SEQ), (b3p, b3s, SEQ))
    xs_rows = nc.dram_tensor("xs_rows", [NSLOT, D], F32, kind="Internal").ap()
    ys_rows = nc.dram_tensor("ys_rows", [NSLOT, D], F32, kind="Internal").ap()
    qa_rows = nc.dram_tensor("qa_rows", [DEC, D], F32, kind="Internal").ap()
    o_rows = [nc.dram_tensor(f"o_rows{g}", [SEQ, 4 * 66], F32, kind="Internal").ap() for g in range(2)]

    q_rows = nc.dram_tensor("q_rows", [NDIL, DEC, NKV, 4 * HD], F32, kind="Internal").ap()

    with ExitStack() as ctx:
        def sb(name, shape, dt=F32, to=ctx):
            return to.enter_context(nc.sbuf_tensor(name, shape, dt))

        live = [[]]

        def sem(name):
            live[-1].append(nc.alloc_semaphore(name=name))
            return live[-1][-1]

        def scoped(stage):
            def run(*args, **kw):
                live.append([])
                stage(*args, **kw)
                nc.clear_and_free_semaphores(live.pop())
                nc.all_engine_barrier()
            return run

        ps = ctx.enter_context(nc.psum_tensor("ps", [128, 8 * 512], F32))

        def bank(b, n=1):
            return ps[:, 512 * b:512 * (b + n)]

        cst = sb("cst", [128, NCONST])
        x = sb("x", [128, NT, D])
        oT = sb("oT", [128, NPAIR, TOK])

        def C(name):
            return cst[:, CONST[name][0]:CONST[name][1]]

        ident, ones = C("ident"), C("ones")
        s_act, s_dve, s_pool = sem("act_steps"), sem("dve_steps"), sem("pool_steps")
        act_do, dve_do, pool_do = Steps(s_act), Steps(s_dve), Steps(s_pool)
        s_const, s_zero, s_zeroed = sem("const_in"), sem("zero_tile"), sem("xs_zeroed")
        s_x = [sem(f"x_in{t}") for t in range(NT)]

        zero = sb("zero", [128, D])
        gain_row = sb("gain_row", [128, D])
        ss, rs = sb("ss", [128, NT]), sb("rs", [128, NT])

        class Norm:
            count = 0

            def __init__(self, gains):
                self.gains, self.k = gains, Norm.count
                Norm.count += 1
                self.gb = [gain_row, zero][:len(gains)]
                self.s_g, self.s_ms, self.s_rstd = (nc.alloc_semaphore(name=f"{n}{self.k}") for n in
                                                    ("gain_in", "meansq_ready", "rstd_ready"))

            def load(self, sp):
                for row, g in zip(self.gb, self.gains):
                    sp.dma_start(row[:, :], g.partition_broadcast(128)).then_inc(self.s_g, 16)

            def square(self, act, t, junk):
                rows = TILES[t][1]
                if t:
                    act.wait_ge(self.s_ms, t)
                elif self.k:
                    act.wait_ge(last_norm[0].s_rstd, NT)
                nc.scalar.activation(junk[0:rows, :], x[0:rows, t, :], ACT.Square, scale=D ** -0.5,
                                     accum_out=ss[0:rows, t:t + 1]).then_inc(self.s_ms, 1)

            def power(self, pool, t):
                rows = TILES[t][1]
                pool.wait_ge(self.s_ms, t + 1)
                mean = ss[0:rows, t:t + 1]
                pool_do(nc.gpsimd.tensor_tensor(mean, mean, C("eps")[0:rows, :], ALU.add))
                nc.gpsimd.tensor_tensor(rs[0:rows, t:t + 1], mean, C("mhalf")[0:rows, 0:1], ALU.pow).then_inc(self.s_rstd, 1)

            def turn(self, outs_T, keep=None, prefetch=None):
                turn_normed(self, outs_T, keep, prefetch)
                last_norm[0] = self

        last_norm = [None]

        @scoped
        def turn_normed(norm, outs_T, keep, prefetch):
            k, gains, s_g, s_rstd = norm.k, norm.gains, norm.s_g, norm.s_rstd
            s_xn, s_tp, s_ev = (sem(f"{n}{k}") for n in ("xn_ready", "xn_turned", "xnT_ready"))
            with ExitStack() as ph, nc.Block() as block:
                xn = keep if keep is not None else sb(f"xn{k}", [128, 2, D], to=ph)
                units = [(t, rows, gi) for t, rows in TILES for gi in range(len(gains))]

                def slot(n, t):
                    return t if keep is not None else n % 2

                @block.sync
                def _(sp):
                    if prefetch:
                        prefetch(sp)

                @block.scalar
                def _(act):
                    for n, (t, rows, gi) in enumerate(units):
                        act.wait_ge(s_tp, n + 1)
                        src = bank(2 * (n % 2), 2).rearrange("p (k m) -> p k m", k=KT)
                        nc.scalar.activation(outs_T[gi][:, :, 128 * t:128 * t + rows], src[:, :, 0:rows],
                                             ACT.Copy).then_inc(s_ev, 1)

                @block.vector
                def _(dve):
                    dve.wait_ge(s_g, 16 * len(gains))
                    for n, (t, rows, gi) in enumerate(units):
                        dve.wait_ge(s_rstd, t + 1)
                        if keep is None and n >= 2:
                            dve.wait_ge(s_tp, n - 1)
                        nc.vector.scalar_tensor_tensor(
                            out=xn[0:rows, slot(n, t), :], in0=x[0:rows, t, :], scalar=rs[0:rows, t:t + 1],
                            in1=norm.gb[gi][0:rows, :], op0=ALU.mult, op1=ALU.mult).then_inc(s_xn, 1)

                @block.tensor
                def _(pe):
                    for n, (t, rows, gi) in enumerate(units):
                        pe.wait_ge(s_xn, n + 1)
                        if n >= 2:
                            pe.wait_ge(s_ev, n - 1)
                        dst = bank(2 * (n % 2), 2).rearrange("p (k m) -> p k m", k=KT)
                        for kt in range(KT):
                            last = nc.tensor.transpose(dst[:, kt, 0:rows],
                                                       xn[0:rows, slot(n, t), kt:D:KT], ident[0:rows, 0:rows])
                        last.then_inc(s_tp, 1)

        norm = Norm([a["g_attn"][0]])
        with ExitStack() as ph, nc.Block() as block:
            junk = sb("junk0", [128, D], to=ph)

            @block.sync
            def _(sp):
                for t, rows in TILES:
                    src = a["x_prompt"][0, 128 * t:128 * t + 128, :] if t < 4 else a["x_sample"][:, 0, :]
                    sp.dma_start(x[0:rows, t, :], src).then_inc(s_x[t], 16)
                    if t == 0:
                        sp.dma_start(cst[:, :], a["const"]).then_inc(s_const, 16)
                norm.load(sp)
                sp.wait_ge(s_const, 16)

            @block.vector
            def _(dve):
                dve.memset(zero[:, :], 0.0).then_inc(s_zero, 1)

            @block.scalar
            def _(act):
                for t in range(NT):
                    act.wait_ge(s_x[t], 16)
                    norm.square(act, t, junk)

            @block.gpsimd
            def _(pool):
                pool_do.on(pool)
                pool.wait_ge(s_const, 16)
                for t in range(NT):
                    norm.power(pool, t)
                pool_do.done()

        class OutProjection:

            def __init__(self, name, w_o, w):
                self.w_o, self.w = w_o, w
                self.s_in, self.s_done, self.s_added = sem(f"wo_in_{name}"), sem(f"oproj_done_{name}"), sem(f"x_added_{name}")

            def load(self, sp, pairs):
                for m in pairs:
                    sp.dma_start(self.w[m], self.w_o[128 * m:128 * m + 128, :]).then_inc(self.s_in, 16)

            def product(self, pe, i):
                t, n = i // 2, i % 2
                rows = TILES[t][1]
                if i == 0:
                    pe.wait_ge(self.s_in, 16 * NPAIR)
                if i >= 2:
                    pe.wait_ge(self.s_added, i - 1)
                for m in range(NPAIR):
                    last = nc.tensor.matmul(bank(6 + n)[0:rows, :], oT[:, m, 128 * t:128 * t + rows],
                                            self.w[m][:, 512 * n:512 * n + 512], start=(m == 0), stop=(m == NPAIR - 1))
                last.then_inc(self.s_done, 1)

            def add(self, dve, i):
                t, n = i // 2, i % 2
                rows = TILES[t][1]
                dve.wait_ge(self.s_done, i + 1)
                xh = x[0:rows, t, 512 * n:512 * n + 512]
                nc.vector.tensor_tensor(xh, xh, bank(6 + n)[0:rows, :], ALU.add).then_inc(self.s_added, 1)

        phA = ExitStack()
        xnT = sb("xnT_a", [128, KT, TOK], to=phA)
        qTs = sb("qTs", [128, NPAIR, DEC], to=phA)
        vres = sb("vres", [128, DEC * NCH, D], to=phA)
        s_vres = sem("past_v_in")
        gidx = sb("gidx", [128, 2, DEC * NCH], I32, to=phA)
        w_qkv = a["w_qkv_a"][0].rearrange("(p t) n -> p t n", t=KT)
        cache_rows = a["cache_kv_a"][0].rearrange("g s c h e -> (g s c) (h e)")
        wA = sb("wA", [128, 3, KT, 128], to=phA)
        s_w = [sem(f"w_{n}_in") for n in "qkv"]

        def first_qkv(sp):
            for m in range(3):
                sp.dma_start(wA[:, m], w_qkv[:, :, m * D:m * D + 128]).then_inc(s_w[m], 16)

        norm.turn([xnT], prefetch=first_qkv)
        wo_hi = sb("wo_hi", [128, NPAIR // 2, D], to=phA)
        out_a = OutProjection("a", a["w_o_a"][0], [flat(xnT)[:, D * m:D * m + D] for m in range(NPAIR // 2)]
                              + [wo_hi[:, m, :] for m in range(NPAIR // 2)])
        OFF = {0: 0, 1: 512, 3: 896, 2: 1024}
        NZ = 1280

        with ExitStack() as ph, nc.Block() as block:
            qkvT = sb("qkvT", [128, 3, TOK], to=ph)
            kv_tok = sb("kv_tok", [128, 2, NT, 128], to=ph)
            bias = sb("bias", [128, NH], to=ph)
            z = sb("z", [128, 2, NZ], to=ph)
            w = sb("w", [128, 2, NZ], to=ph)
            spl = sb("spl", [128, 2, NZ], to=ph)
            U = sb("U", [128, 2, 384], to=ph)
            ptab = sb("ptab", [128, DEC * NCH], I32, to=ph)
            ptf = sb("ptf", [128, 2, DEC * NCH], to=ph)
            s_bias, s_pt, s_idx = sem("bias_in"), sem("pages_in"), sem("row_index_ready")
            s_proj, s_pev, s_qk, s_zev = sem("proj_done"), sem("proj_copied"), sem("scores_done"), sem("z_ready")
            s_abs, s_log, s_sp, s_spm = sem("abs_ready"), sem("log_ready"), sem("softplus_ready"), sem("softplus_masked")
            s_c, s_t, s_tm, s_a = sem("tails_done"), sem("logw_ready"), sem("logw_masked"), sem("weights_ready")
            s_av, s_oev, s_kvt, s_kve, s_kvo = (sem("av_done"), sem("av_copied"), sem("kv_turned"),
                                                sem("kv_tok_ready"), sem("kv_stored"))
            s_qs = sem("sample_q_kept")

            @block.sync
            def _(sp):
                sp.dma_start(bias[:, :], a["sb_bias"][0].partition_broadcast(128)).then_inc(s_bias, 16)
                sp.dma_start(ptab[:, :], a["page_table"].rearrange("b c -> (b c)").partition_broadcast(128)).then_inc(s_pt, 16)

                def body(n, last):
                    if not last:
                        for m in range(3):
                            sp.wait_ge(s_proj, 6 * n + 2 * m + 2)
                            sp.dma_start(wA[:, m], w_qkv[:, :, ds(m * D + 128 * (n + 1), 128)]).then_inc(s_w[m], 16)
                    sp.wait_ge(s_kve, 4 * n + 4)
                    for c in range(2):
                        dst_p = a_prompt[0, 0].rearrange("(t p) c h e -> p t c (h e)", p=128)
                        sp.dma_start(dst_p[:, :, c, ds(128 * n, 128)], kv_tok[:, c, 0:4, :]).then_inc(s_kvo, 16)
                        dst_s = a_sample[0, :, 0].rearrange("b c h e -> b c (h e)")
                        sp.dma_start(dst_s[:, c, ds(128 * n, 128)], kv_tok[0:DEC, c, 4, :]).then_inc(s_kvo, 16)

                sp.nop().then_inc(s_oev, 1)
                out_a.load(sp, range(NPAIR // 2, NPAIR))
                with sp.Fori(0, NPAIR - 1) as n:
                    body(n, False)
                sp.wait_ge(s_proj, 6 * NPAIR)
                out_a.load(sp, range(NPAIR // 2))
                body(NPAIR - 1, True)
                sp.wait_ge(s_kvo, 64 * NPAIR)

            def project(pe, m, n):
                pe.wait_ge(s_w[m], 16 * n + 16)
                if m == 0:
                    pe.wait_ge(s_kve, 4 * n)
                if m == 2:
                    pe.wait_ge(s_kve, 4 * n + 2)
                for h in range(2):
                    if m == 1:
                        pe.wait_ge(s_pev, 6 * n + h + 1)
                    for k in range(KT):
                        last = nc.tensor.matmul(bank(6 + h)[:, 0:HALF], wA[:, m, k, :],
                                                xnT[:, k, HALF * h:HALF * h + HALF],
                                                start=(k == 0), stop=(k == KT - 1))
                    last.then_inc(s_proj, 1)

            def turn_kv(pe, c, n):
                pe.wait_ge(s_pev, 6 * n + 4 + 2 * c)
                for t, rows in TILES:
                    last = nc.tensor.transpose(ps[0:rows, 512 * 6 + 128 * t:512 * 6 + 128 * t + 128],
                                               qkvT[:, 1 + c, 128 * t:128 * t + rows], ident)
                last.then_inc(s_kvt, 1)

            @block.tensor
            def _(pe):
                project(pe, 0, 0)
                project(pe, 1, 0)
                turn_kv(pe, 0, 0)
                project(pe, 2, 0)
                turn_kv(pe, 1, 0)

                def body(n, last_pair):
                    for h in range(2):
                        if h:
                            pe.wait_ge(s_oev, n + 1)
                        r = slice(64 * h, 64 * h + 64)
                        for c in range(4):
                            o = 1536 * h + OFF[c]
                            last = nc.tensor.matmul(ps[:, o:o + 512 - 128 * c], qkvT[r, 1, 128 * c:128 * c + 128],
                                                    qkvT[r, 0, 128 * c:512], start=True, stop=True)
                        last.then_inc(s_qk, 1)
                    if not last_pair:
                        project(pe, 0, n + 1)
                        project(pe, 1, n + 1)
                    for h in range(2):
                        if h and not last_pair:
                            turn_kv(pe, 0, n + 1)
                        pe.wait_ge(s_spm, 2 * n + h + 1)
                        b = 1536 * h

                        def mm(lhs, rhs, o, start, stop, width):
                            return nc.tensor.matmul(ps[:, b + o:b + o + width], lhs, rhs, start=start, stop=stop,
                                                    skip_group_check=True)

                        S = spl[:, h, :]
                        tri = C("tri")
                        mm(tri, S[:, 0:512], 0, True, False, 512)
                        mm(ones, S[:, 512:640], 128, False, False, 128)
                        mm(ones, U[:, h, 128:384], 256, False, True, 256)
                        mm(tri, S[:, 512:896], 512, True, False, 384)
                        mm(ones, S[:, 1024:1152], 640, False, False, 128)
                        mm(ones, U[:, h, 0:128], 768, False, True, 128)
                        mm(tri, S[:, 896:1024], 896, True, True, 128)
                        mm(tri, S[:, 1024:1280], 1024, True, False, 256)
                        mm(ones, S[:, 896:1024], 1152, False, True, 128).then_inc(s_c, 1)
                    if not last_pair:
                        project(pe, 2, n + 1)
                    pe.wait_ge(s_t, 2 * n + 2)
                    for h in range(2):
                        pe.wait_ge(s_a, 2 * n + h + 1)
                        for c in range(4):
                            last = nc.tensor.matmul(bank(3)[64 * h:64 * h + 64, 128 * c:512],
                                                    kv_tok[:, 1, c, 64 * h:64 * h + 64],
                                                    w[:, h, OFF[c]:OFF[c] + 512 - 128 * c],
                                                    start=(c == 0), stop=(c == 3), skip_group_check=True)
                    last.then_inc(s_av, 1)
                    if not last_pair:
                        turn_kv(pe, 1, n + 1)

                with pe.Fori(0, NPAIR - 1) as n:
                    body(n, False)
                body(NPAIR - 1, True)

            @block.scalar
            def _(act):
                act_do.on(act)

                def proj_copy(m, n, h):
                    act.wait_ge(s_proj, 6 * n + 2 * m + h + 1)
                    if m == 0:
                        act.wait_ge(s_qs, n)
                    nc.scalar.activation(qkvT[:, m, HALF * h:HALF * h + HALF], bank(6 + h)[:, 0:HALF],
                                         ACT.Copy).then_inc(s_pev, 1)

                for m in range(3):
                    for h in range(2):
                        proj_copy(m, 0, h)
                act.wait_ge(s_bias, 16)

                def body(n, last_pair):
                    for h in range(2):
                        act.wait_ge(s_qk, 2 * n + h + 1)
                        nc.scalar.activation(z[:, h, :], ps[:, 1536 * h:1536 * h + NZ], ACT.Identity,
                                             bias=bias[:, ds(2 * n + h, 1)], scale=SCALE).then_inc(s_zev, 1)
                    for h in range(2):
                        act.wait_ge(s_abs, 2 * n + h + 1)
                        act_do(nc.scalar.activation(w[:, h, :], w[:, h, :], ACT.Exp))
                    if not last_pair:
                        proj_copy(0, n + 1, 0)
                    for h in range(2):
                        nc.scalar.activation(w[:, h, :], w[:, h, :], ACT.Ln, bias=1.0).then_inc(s_log, 1)
                    if not last_pair:
                        proj_copy(0, n + 1, 1)
                        for h in range(2):
                            proj_copy(1, n + 1, h)
                    for h in range(2):
                        act.wait_ge(s_tm, 2 * n + h + 1)
                        nc.scalar.activation(w[:, h, :], w[:, h, :], ACT.Exp).then_inc(s_a, 1)
                    if not last_pair:
                        for h in range(2):
                            proj_copy(2, n + 1, h)

                with act.Fori(0, NPAIR - 1) as n:
                    act_do.enter(n, 2)
                    body(n, False)
                act_do.leave(NPAIR - 1)
                act_do.enter(0, 2)
                body(NPAIR - 1, True)
                act_do.leave(1)

            @block.vector
            def _(dve):
                dve_do.on(dve)
                dve.wait_ge(s_pt, 16)
                dve_do(nc.vector.tensor_copy(ptf[:, 0, :], ptab[:, :]))
                dve_do(nc.vector.tensor_scalar(ptf[:, 0, :], ptf[:, 0, :], 2.0 * PAGE, C("pidx"), ALU.mult, ALU.add))
                dve_do(nc.vector.tensor_scalar(ptf[:, 1, :], ptf[:, 0, :], 1.0, None, ALU.add))
                nc.vector.tensor_copy(gidx[:, :, :], ptf[:, :, :]).then_inc(s_idx, 1)
                dve_do.done()

                def kv_copy(n, c):
                    dve.wait_ge(s_kvo, 64 * n)
                    dve.wait_ge(s_kvt, 2 * n + c + 1)
                    nc.vector.tensor_copy(flat(kv_tok[:, c, 0:4, :]), bank(6)).then_inc(s_kve, 1)
                    nc.vector.tensor_copy(kv_tok[0:DEC, c, 4, :], bank(7)[0:DEC, 0:128]).then_inc(s_kve, 1)

                def q_keep(n):
                    dve.wait_ge(s_pev, 6 * n + 2)
                    nc.vector.tensor_copy(qTs[:, ds(n, 1), :], qkvT[:, 0:1, SEQ:TOK]).then_inc(s_qs, 1)

                q_keep(0)
                kv_copy(0, 0)
                kv_copy(0, 1)

                def body(n, last_pair):
                    for h in range(2):
                        dve.wait_ge(s_zev, 2 * n + h + 1)
                        nc.vector.scalar_tensor_tensor(out=w[:, h, :], in0=z[:, h, :], scalar=-1.0, in1=z[:, h, :],
                                                       op0=ALU.mult, op1=ALU.min).then_inc(s_abs, 1)
                    for h in range(2):
                        dve.wait_ge(s_log, 2 * n + h + 1)
                        nc.vector.scalar_tensor_tensor(out=spl[:, h, :], in0=z[:, h, :], scalar=0.0, in1=w[:, h, :],
                                                       op0=ALU.max, op1=ALU.add).then_inc(s_sp, 1)
                    if not last_pair:
                        q_keep(n + 1)
                    for h in range(2):
                        dve.wait_ge(s_c, 2 * n + h + 1)
                        nc.vector.tensor_tensor(w[:, h, :], z[:, h, :], ps[:, 1536 * h:1536 * h + NZ],
                                                ALU.subtract).then_inc(s_t, 1)
                        if h == 0 and not last_pair:
                            kv_copy(n + 1, 0)
                    dve.wait_ge(s_av, n + 1)
                    nc.vector.tensor_copy(oT[:, ds(n, 1), 0:512],
                                          bank(3).rearrange("p (a m) -> p a m", a=1)).then_inc(s_oev, 1)
                    if not last_pair:
                        kv_copy(n + 1, 1)

                with dve.Fori(0, NPAIR - 1) as n:
                    body(n, False)
                body(NPAIR - 1, True)

            @block.gpsimd
            def _(pool):
                pool_do.on(pool)
                pool.wait_ge(s_idx, 1)
                for u in range(DEC * NCH):
                    pool.indirect_dma_start(out=vres[:, u, :], out_offset=None, in_=cache_rows,
                                            in_offset=bass.IndirectOffsetOnAxis(ap=gidx[:, 1, u:u + 1], axis=0)
                                            ).then_inc(s_vres, 16)

                def diagonal(t, mask, op):
                    for c in range(4):
                        v = t[:, OFF[c]:OFF[c] + 128]
                        last = nc.gpsimd.tensor_tensor(v, v, mask, op)
                        if c < 3:
                            pool_do(last)
                    return last

                def body(n):
                    for h in range(2):
                        pool.wait_ge(s_sp, 2 * n + h + 1)
                        S = spl[:, h, :]
                        pool_do(diagonal(S, C("strict"), ALU.mult))
                        pool_do(nc.gpsimd.tensor_tensor(U[:, h, 0:128], S[:, 1152:1280], S[:, 896:1024], ALU.add))
                        pool_do(nc.gpsimd.tensor_tensor(U[:, h, 128:256], S[:, 640:768], S[:, 1024:1152], ALU.add))
                        nc.gpsimd.tensor_tensor(U[:, h, 256:384], S[:, 768:896], U[:, h, 0:128],
                                                ALU.add).then_inc(s_spm, 1)
                    for h in range(2):
                        pool.wait_ge(s_t, 2 * n + h + 1)
                        diagonal(w[:, h, :], C("m3"), ALU.add).then_inc(s_tm, 1)

                with pool.Fori(0, NPAIR) as n:
                    pool_do.enter(n, 2 * 6 + 2 * 3)
                    body(n)
                pool_do.leave(NPAIR)

        with ExitStack() as ph, nc.Block() as block:
            kpast = sb("kpast", [128, 3, D], to=ph)
            qrow = sb("qrow", [DEC, D], to=ph)
            qb = wA[:, :, :, :].rearrange("p m k n -> p m (k n)")
            prod = sb("prod", [128, D], to=ph)
            junk = sb("junk1", [128, D], to=ph)
            norm = Norm([a["g_ffn"][0]])
            oh_a = sb("oh_a", [128, 2, D], to=ph)
            biasb = sb("biasb", [128, NH], to=ph)
            zs = sb("zs", [128, NCH, DEC, NH], to=ph)
            ws = sb("ws", [128, NCH * 128], to=ph)
            sps = sb("sps", [128, NCH * 128], to=ph)
            s_k = [sem(f"past_k_in{i}") for i in range(3)]
            s_b, s_qt, s_qr, s_z, s_e, s_zz, s_lg, s_so, s_ct, s_lw, s_wt, s_pv, s_fin = (
                sem(n) for n in ("sbias_in", "sq_turned", "sq_rows", "sz_done", "sprod_done", "sz_ready",
                                 "slog_ready", "ssoftplus", "stails", "slogw", "sweights", "spv_done", "so_ready"))
            s_qst, s_qin = sem("sq_stored"), [sem(f"sq_in{i}") for i in range(QSLOTS)]
            s_oh0, s_ohc, s_ot = sem("sheads_zeroed"), sem("sheads_copied"), sem("sheads_turned")
            units = [(b, c) for b in range(DEC) for c in range(NCH)]

            @block.sync
            def _(sp):
                sp.dma_start(biasb[:, :], a["sb_bias"][0].partition_broadcast(128)).then_inc(s_b, 16)
                sp.wait_ge(s_qr, 1)
                sp.dma_start(qa_rows, qrow[:, :]).then_inc(s_qst, 16)
                sp.wait_ge(s_qst, 16)
                for b in range(DEC):
                    if b >= QSLOTS:
                        sp.wait_ge(s_e, NCH * (b - QSLOTS + 1))
                    sp.dma_start(qb[:, b % QSLOTS, :], qa_rows[b].partition_broadcast(128)).then_inc(s_qin[b % QSLOTS], 16)
                norm.load(sp)
                sp.wait_ge(s_zero, 1)
                sp.wait_ge(s_e, len(units) - 2)
                with sp.Fori(0, NSLOT // 128) as i:
                    sp.dma_start(xs_rows[ds(i * 128, 128), :], zero[:, :]).then_inc(s_zeroed, 16)
                with sp.Fori(NE * CAP // 128, NSLOT // 128) as i:
                    sp.dma_start(ys_rows[ds(i * 128, 128), :], zero[:, :]).then_inc(s_zeroed, 16)

            @block.gpsimd
            def _(pool):
                for u in range(len(units)):
                    if u >= 3:
                        pool.wait_ge(s_e, u - 2)
                    pool.indirect_dma_start(out=kpast[:, u % 3, :], out_offset=None, in_=cache_rows,
                                            in_offset=bass.IndirectOffsetOnAxis(ap=gidx[:, 0, u:u + 1], axis=0)
                                            ).then_inc(s_k[u % 3], 16)
                pool_do.on(pool)
                for t in range(NT):
                    norm.power(pool, t)
                pool_do.done()

            @block.tensor
            def _(pe):
                for k in range(NPAIR):
                    last = nc.tensor.transpose(ps[0:DEC, 128 * k:128 * k + 128], qTs[:, k, :], ident)
                last.then_inc(s_qt, 1)
                for i in range(8):
                    out_a.product(pe, i)
                pe.wait_ge(s_so, 1)
                nc.tensor.matmul(bank(0)[:, 0:128], C("tri"), sps[:, 0:128], start=True, stop=False, skip_group_check=True)
                nc.tensor.matmul(bank(0)[:, 0:128], ones, sps[:, 128:256], start=False, stop=True, skip_group_check=True)
                nc.tensor.matmul(bank(0)[:, 128:256], C("tri"), sps[:, 128:256], start=True, stop=True,
                                 skip_group_check=True).then_inc(s_ct, 1)
                pe.wait_ge(s_wt, 1)
                pe.wait_ge(s_vres, 16 * len(units))
                wv = ws[:, :].rearrange("p (c b h) -> p c b h", c=NCH, b=DEC)
                for b in range(DEC):
                    for n in range(2):
                        for c in range(NCH):
                            last = nc.tensor.matmul(bank(2 + 2 * (b // 4) + n)[32 * (b % 4):32 * (b % 4) + NH, :], wv[:, c, b, :],
                                                    vres[:, NCH * b + c, 512 * n:512 * n + 512], start=(c == 0), stop=(c == NCH - 1))
                    if b % 4 == 3:
                        last.then_inc(s_pv, 1)
                for q in range(2):
                    pe.wait_ge(s_ohc, 8 * q + 8)
                    for h in range(NH):
                        o = 8 * (h // 2) + 4 * q
                        last = nc.tensor.matmul(bank(1)[64 * (h % 2):64 * (h % 2) + 64, o:o + 4], oh_a[:, q, HD * h:HD * h + HD],
                                                ident[:, h:128:32], start=True, stop=True)
                last.then_inc(s_ot, 1)
                pe.wait_ge(s_fin, 1)
                for i in (8, 9):
                    out_a.product(pe, i)

            @block.vector
            def _(dve):
                dve_do.on(dve)
                dve.wait_ge(s_qt, 1)
                nc.vector.tensor_copy(qrow[:, :], ps[0:DEC, 0:1024]).then_inc(s_qr, 1)
                nc.vector.memset(flat(oh_a), 0.0).then_inc(s_oh0, 1)
                for u, (b, c) in enumerate(units):
                    dve.wait_ge(s_k[u % 3], 16 * (u // 3 + 1))
                    dve.wait_ge(s_qin[b % QSLOTS], 16 * (b // QSLOTS + 1))
                    nc.vector.tensor_tensor(prod[:, :], kpast[:, u % 3, :], qb[:, b % QSLOTS, :], ALU.mult).then_inc(s_e, 1)
                    dve.wait_ge(s_e, u + 1)
                    nc.vector.reduce_sum(zs[:, c, b, :], prod[:, :].rearrange("p (h e) -> p h e", e=HD), AX_X).then_inc(s_z, 1)
                    dve.wait_ge(s_z, u + 1)
                    if c == NCH - 1 and b >= 1:
                        out_a.add(dve, b - 1)
                dve.wait_ge(s_b, 16)
                zf = zs[:, :, :, :].rearrange("p c b h -> p (c b) h")
                zw = zs[:, :, :, :].rearrange("p c b h -> p (c b h)")
                dve_do(nc.vector.tensor_scalar(zw, zw, SCALE, None, ALU.mult))
                dve_do(nc.vector.tensor_tensor(zf, zf, biasb[:, :].unsqueeze(1).to_broadcast([128, NCH * DEC, NH]), ALU.add))
                nc.vector.scalar_tensor_tensor(out=ws[:, :], in0=zw, scalar=-1.0, in1=zw, op0=ALU.mult,
                                               op1=ALU.min).then_inc(s_zz, 1)
                out_a.add(dve, DEC - 1)
                dve.wait_ge(s_lg, 1)
                nc.vector.scalar_tensor_tensor(out=sps[:, :], in0=zw, scalar=0.0, in1=ws[:, :], op0=ALU.max,
                                               op1=ALU.add).then_inc(s_so, 1)
                dve.wait_ge(s_ct, 1)
                nc.vector.tensor_tensor(ws[:, :], zw, bank(0)[:, 0:256], ALU.subtract).then_inc(s_lw, 1)
                dve.wait_ge(s_oh0, 1)
                for q in range(2):
                    dve.wait_ge(s_pv, q + 1)
                    for i in range(4):
                        for n in range(2):
                            rows = slice(32 * i, 32 * i + NH)
                            nc.vector.tensor_copy(oh_a[rows, q, 512 * n:512 * n + 512], bank(2 + 2 * q + n)[rows, :]).then_inc(s_ohc, 1)
                dve.wait_ge(s_ot, 1)
                nc.vector.tensor_copy(oT[:, :, SEQ:TOK], bank(1)[:, 0:DEC * NPAIR].rearrange("p (n b) -> p n b", b=DEC)).then_inc(s_fin, 1)
                for i in (8, 9):
                    out_a.add(dve, i)
                dve_do.done()

            @block.scalar
            def _(act):
                act_do.on(act)

                def square(t):
                    act.wait_ge(out_a.s_added, 2 * t + 2)
                    norm.square(act, t, junk)

                for t in range(3):
                    square(t)
                act.wait_ge(s_zz, 1)
                act_do(nc.scalar.activation(ws[:, :], ws[:, :], ACT.Exp))
                nc.scalar.activation(ws[:, :], ws[:, :], ACT.Ln, bias=1.0).then_inc(s_lg, 1)
                act.wait_ge(s_lw, 1)
                nc.scalar.activation(ws[:, :], ws[:, :], ACT.Exp).then_inc(s_wt, 1)
                act_do.done()
                square(3)
                square(4)
        phA.close()

        def open_ring(sp, sems):
            for s in sems:
                sp.nop().then_inc(s, 1)

        @scoped
        def moe(layer, norm, next_norm):
            L = str(layer)

            def lsem(n):
                return sem(f"{n}_{L}")

            pos_i = sb("pos_i" + L, [128, 2, NT], I32, to=phM)
            wts = sb("wts" + L, [128, 2, NT], to=phM)
            over_i = sb("over_i" + L, [1, NOVER + 1], I32, to=phM)
            s_disp = lsem("rows_placed")
            wg = [sb(f"wg{s}_" + L, [128, KT, FE], to=phM) for s in range(WSLOTS)]
            wu = [sb(f"wu{s}_" + L, [128, KT, FE], to=phM) for s in range(WSLOTS)]
            wd = [sb(f"wd{s}_" + L, [128, 2, D], to=phM) for s in range(WSLOTS)]
            s_in = [lsem(f"block_in{s}") for s in range(WSLOTS)]

            def load_weights(eng, s, e, sig):
                eng.dma_start(wg[s][:, :, :], a["w_gate"][layer, ds(e, 1)].rearrange("a (p t) f -> p (a t) f", t=KT)).then_inc(sig, 16)
                eng.dma_start(wu[s][:, :, :], a["w_up"][layer, ds(e, 1)].rearrange("a (p t) f -> p (a t) f", t=KT)).then_inc(sig, 16)
                eng.dma_start(wd[s][:, :, :], a["w_down"][layer, ds(e, 1)].rearrange("a (p t) d -> p (a t) d", t=2)).then_inc(sig, 16)

            def load_rows(eng, s, row0, sig):
                eng.dma_start(xs[s][:, :], xs_rows[ds(row0, CAP), :]).then_inc(sig, 16)

            def first_weights(sp):
                for s in range(WSLOTS):
                    load_weights(sp, s, s, s_in[s])

            with ExitStack() as ph:
                xn = sb("xn_m" + L, [128, NT, D], to=ph)
                xnT = sb("xnT_m" + L, [128, KT, TOK], to=ph)
                wr = sb("wr" + L, [128, KT, NG + NE], to=ph)
                rb = sb("rb" + L, [128, NG + NE], to=ph)
                lg = sb("lg" + L, [128, NT, NG + NE], to=ph)
                st = sb("st" + L, [128, 12, NT], to=ph)
                g4 = sb("g4" + L, [128, 3, NT, NG], to=ph)
                el = sb("el" + L, [128, NT, NE], to=ph)
                oh = sb("oh" + L, [128, 3, NT, NE], to=ph)
                tmp = sb("tmp" + L, [128, NT, NE], to=ph)
                rank = sb("rank" + L, [128, NT, NE], to=ph)
                nov = sb("nov" + L, [NE, 2, 128], to=ph)
                ovb = sb("ovb" + L, [128, NE + 1], to=ph)
                far = sb("far" + L, [128, NE], to=ph)
                ovm = sb("ovm" + L, [1, NOVER, NE], to=ph)
                ovf = sb("ovf" + L, [1, NOVER + 1], to=ph)
                s_r, s_l, s_ex, s_gx, s_oh, s_rk, s_nv, s_ob, s_pos = (
                    lsem(n) for n in ("router_in", "logits_done", "exp_in", "exp_ready", "onehot_ready", "ranks_done",
                                      "over_counted", "over_base", "slots_ready"))
                run = sb("run" + L, [128, NT, NE], to=ph)

                def routers_first(sp):
                    sp.dma_start(wr[:, :, 0:NG], a["w_router_group"][layer].rearrange("(p t) n -> p t n", t=KT)).then_inc(s_r, 16)
                    sp.dma_start(wr[:, :, NG:], a["w_router_expert"][layer].rearrange("(p t) n -> p t n", t=KT)).then_inc(s_r, 16)
                    sp.dma_start(rb[:, 0:NG], a["b_router_group"][layer].partition_broadcast(128)).then_inc(s_r, 16)
                    sp.dma_start(rb[:, NG:], a["b_router_expert"][layer].partition_broadcast(128)).then_inc(s_r, 16)
                    first_weights(sp)

                norm.turn([xnT], keep=xn, prefetch=routers_first)

                with nc.Block() as block:
                    @block.tensor
                    def _(pe):
                        pe.wait_ge(s_r, 64)
                        for t, rows in TILES:
                            for k in range(KT):
                                last = nc.tensor.matmul(ps[0:rows, 64 * t:64 * t + NG + NE], xnT[:, k, 128 * t:128 * t + rows],
                                                        wr[:, k, :], start=(k == 0), stop=(k == KT - 1))
                        last.then_inc(s_l, 1)
                        pe.wait_ge(s_oh, 1)
                        nc.tensor.matmul(bank(1)[:, 0:NT * NE], C("strict"), flat(oh[:, 2]), start=True, stop=False, skip_group_check=True)
                        nc.tensor.matmul(bank(1)[:, NE:NT * NE], ones, flat(run[:, 0:NT - 1]), start=False, stop=True,
                                         skip_group_check=True)
                        nc.tensor.matmul(bank(2)[0:NE, 0:128], run[:, NT - 1, :], ones, start=True, stop=True).then_inc(s_rk, 1)
                        pe.wait_ge(s_nv, 1)
                        nc.tensor.matmul(bank(3)[:, 0:NE + 1], nov[:, 1, :], C("strict")[0:NE, 0:NE + 1],
                                         start=True, stop=True).then_inc(s_ob, 1)

                    @block.scalar
                    def _(act):
                        act.wait_ge(s_ex, 1)
                        nc.scalar.activation(g4[:, 2], g4[:, 2], ACT.Exp).then_inc(s_gx, 1)
                        act.wait_ge(s_ex, 2)
                        nc.scalar.activation(st[:, 6, :], st[:, 6, :], ACT.Exp).then_inc(s_gx, 1)

                    @block.vector
                    def _(dve):
                        dve_do.on(dve)
                        V = nc.vector

                        def over(s, n):
                            return st[:, s, :].unsqueeze(2).to_broadcast([128, NT, n])

                        def row(name, n):
                            return C(name)[:, 0:n].unsqueeze(1).to_broadcast([128, NT, n])

                        def first(dst, src, n, mx, ix, eq):
                            dve_do(V.tensor_reduce(st[:, mx, :], src, AX_X, ALU.max))
                            dve_do(V.tensor_tensor(eq, src, over(mx, n), ALU.is_equal))
                            dve_do(V.scalar_tensor_tensor(out=eq, in0=eq, scalar=-99.0, in1=row("iota99", n),
                                                          op0=ALU.mult, op1=ALU.add))
                            dve_do(V.tensor_reduce(st[:, ix, :], eq, AX_X, ALU.min))
                            dve_do(V.tensor_tensor(dst, row("iota", n), over(ix, n), ALU.is_equal))

                        dve_do(V.memset(lg[:, :, :], 0.0))
                        dve.wait_ge(s_l, 1)
                        for t, rows in TILES:
                            dve_do(V.tensor_tensor(lg[0:rows, t, :], ps[0:rows, 64 * t:64 * t + NG + NE], rb[0:rows, :], ALU.add))
                        gl = lg[:, :, 0:NG]
                        first(g4[:, 0], gl, NG, 0, 1, g4[:, 1])
                        V.tensor_tensor(g4[:, 2], gl, over(0, NG), ALU.subtract).then_inc(s_ex, 1)
                        dve_do(V.tensor_scalar(g4[:, 1], g4[:, 0], -NEG, NEG, ALU.mult, ALU.add))
                        dve_do(V.tensor_tensor(el[:, :, :].rearrange("p t (g e) -> p t g e", g=NG),
                                               lg[:, :, NG:].rearrange("p t (g e) -> p t g e", g=NG),
                                               g4[:, 1].unsqueeze(3).to_broadcast([128, NT, NG, EPG]), ALU.add))
                        first(oh[:, 0], el[:, :, :], NE, 2, 3, tmp[:, :, :])
                        dve_do(V.scalar_tensor_tensor(out=el[:, :, :], in0=oh[:, 0], scalar=3 * NEG, in1=el[:, :, :],
                                                      op0=ALU.mult, op1=ALU.add))
                        first(oh[:, 1], el[:, :, :], NE, 4, 5, tmp[:, :, :])
                        V.tensor_tensor(st[:, 6, :], st[:, 4, :], st[:, 2, :], ALU.subtract).then_inc(s_ex, 1)
                        for k in range(2):
                            dve_do(V.tensor_tensor(oh[:, k], oh[:, k],
                                                   C("valid").unsqueeze(2).to_broadcast([128, NT, NE]), ALU.mult))
                        dve_do(V.tensor_tensor(oh[:, 2], oh[:, 0], oh[:, 1], ALU.add))
                        dve_do(V.tensor_copy(run[:, 0], oh[:, 2, 0, :]))
                        for t in range(1, NT):
                            ins = V.tensor_tensor(run[:, t], run[:, t - 1], oh[:, 2, t, :], ALU.add)
                            if t < NT - 1:
                                dve_do(ins)
                        ins.then_inc(s_oh, 1)
                        dve.wait_ge(s_gx, 2)
                        dve_do(V.reduce_sum(st[:, 7, :], g4[:, 2], AX_X))
                        dve_do(V.tensor_scalar(st[:, 8, :], st[:, 6, :], 1.0, None, ALU.add))
                        dve_do(V.tensor_tensor(st[:, 7, :], st[:, 7, :], st[:, 8, :], ALU.mult))
                        dve_do(V.reciprocal(wts[:, 0, :], st[:, 7, :]))
                        dve_do(V.tensor_tensor(wts[:, 1, :], wts[:, 0, :], st[:, 6, :], ALU.mult))
                        dve.wait_ge(s_rk, 1)
                        dve_do(V.tensor_copy(rank[:, :, :].rearrange("p t e -> p (t e)"), bank(1)[:, 0:NT * NE]))
                        dve_do(V.tensor_copy(nov[:, 0, :], bank(2)[0:NE, 0:128]))
                        dve_do(V.memset(nov[:, 1, :], 0.0))
                        blocks = -(-TOK // CAP)
                        for m in range(1, blocks):
                            ins = V.scalar_tensor_tensor(out=nov[:, 1, :], in0=nov[:, 0, :], scalar=float(CAP * m), in1=nov[:, 1, :],
                                                         op0=ALU.is_gt, op1=ALU.add)
                            if m < blocks - 1:
                                dve_do(ins)
                        ins.then_inc(s_nv, 1)
                        dve.wait_ge(s_ob, 1)
                        dve_do(V.tensor_copy(ovb[:, :], bank(3)[:, 0:NE + 1]))
                        dve_do(V.scalar_tensor_tensor(out=far[:, :], in0=ovb[:, 0:NE], scalar=float(CAP), in1=C("ecap"),
                                                      op0=ALU.mult, op1=ALU.subtract))
                        dve_do(V.tensor_scalar(far[:, :], far[:, :], float((NE - 1) * CAP), None, ALU.add))
                        dve_do(V.scalar_tensor_tensor(out=tmp[:, :, :], in0=rank[:, :, :], scalar=float(CAP),
                                                      in1=far[:, :].unsqueeze(1).to_broadcast([128, NT, NE]),
                                                      op0=ALU.is_ge, op1=ALU.mult))
                        dve_do(V.tensor_tensor(rank[:, :, :], rank[:, :, :], tmp[:, :, :], ALU.add))
                        dve_do(V.tensor_tensor(rank[:, :, :], rank[:, :, :], row("ecap", NE), ALU.add))
                        for k in range(2):
                            dve_do(V.tensor_tensor(tmp[:, :, :], rank[:, :, :], oh[:, k], ALU.mult))
                            dve_do(V.reduce_sum(st[:, 9 + k, :], tmp[:, :, :], AX_X))
                        V.tensor_copy(pos_i[:, :, :], st[:, 9:11, :]).then_inc(s_pos, 1)
                        dve_do(V.tensor_tensor(ovm[:, :, :], ovb[0:1, 1:NE + 1].unsqueeze(1).to_broadcast([1, NOVER, NE]),
                                               C("iota")[0:1, 0:NOVER].unsqueeze(2).to_broadcast([1, NOVER, NE]), ALU.is_le))
                        dve_do(V.reduce_sum(ovf[:, 0:NOVER], ovm[:, :, :], AX_X))
                        dve_do(V.tensor_scalar(ovf[:, 0:NOVER], ovf[:, 0:NOVER], float(NE - 1), None, ALU.min))
                        dve_do(V.tensor_copy(ovf[:, NOVER:NOVER + 1], ovb[0:1, NE:NE + 1]))
                        dve_do(V.tensor_copy(over_i[:, :], ovf[:, :]))
                        dve_do.done()

                    @block.gpsimd
                    def _(pool):
                        pool.wait_ge(s_pos, 1)
                        pool.wait_ge(s_zeroed, 16 * (2 * NSLOT // 128 - NE * CAP // 128))
                        for k in range(2):
                            for t, rows in TILES:
                                pool.indirect_dma_start(out=xs_rows, out_offset=bass.IndirectOffsetOnAxis(
                                    ap=pos_i[0:rows, k, t:t + 1], axis=0), in_=xn[0:rows, t, :], in_offset=None).then_inc(s_disp, 16)
                        pool.wait_ge(s_disp, 32 * NT)

            with ExitStack() as ph, nc.Block() as block:
                xs = [sb(f"xs{s}_" + L, [CAP, D], to=ph) for s in range(WSLOTS)]
                xsT = [sb(f"xsT{s}_" + L, [128, KT, CAP], to=ph) for s in range(2)]
                sg = sb("sg" + L, [128, 2, 2, CAP], to=ph)
                hT = sb("hT" + L, [128, 2, 2, CAP], to=ph)
                ysb = [sb(f"ysb{s}_" + L, [CAP, D], to=ph) for s in range(WSLOTS)]
                s_xt = [lsem(f"xs_turned{s}") for s in range(2)]
                s_xe = [lsem(f"xsT_ready{s}") for s in range(2)]
                s_gu = [lsem(f"gate_up_done{s}") for s in range(2)]
                s_si = [lsem(f"silu_ready{s}") for s in range(2)]
                s_h = [lsem(f"h_ready{s}") for s in range(2)]
                s_dn = [lsem(f"down_done{s}") for s in range(WSLOTS)]
                s_ye = [lsem(f"y_copied{s}") for s in range(2)]
                s_yo = [lsem(f"y_stored{s}") for s in range(WSLOTS)]
                o_in, o_xt, o_xe, o_gu, o_si, o_h, o_dn, o_ye, o_yo = (
                    lsem("over_" + n) for n in ("in", "turned", "xsT", "gate_up", "silu", "h", "down", "copied", "stored"))
                s_end = lsem("over_all_stored")
                ROUNDS = NE // WSLOTS

                def load(eng, s, e, row0, sig):
                    load_weights(eng, s, e, sig)
                    load_rows(eng, s, row0, sig)

                def turn_rows(pe, s, q, sig, product=False):
                    for k in range(KT):
                        out, rows = bank(2)[:, CAP * k:CAP * k + CAP], xs[s][:, k:D:KT]
                        if product:
                            last = nc.tensor.matmul(out, rows, ident[0:CAP, 0:CAP], start=True, stop=True)
                        else:
                            last = nc.tensor.transpose(out, rows, ident[0:CAP, 0:CAP])
                    last.then_inc(sig, 1)

                def gate_up(pe, s, q, f, sig):
                    for j, wt in enumerate((wg[s], wu[s])):
                        for k in range(KT):
                            last = nc.tensor.matmul(bank(f)[:, CAP * j:CAP * j + CAP], wt[:, k, f:FE:2],
                                                    xsT[q][:, k, :], start=(k == 0), stop=(k == KT - 1))
                    last.then_inc(sig, 1)

                def down(pe, s, q, f):
                    for n in range(2):
                        last = nc.tensor.matmul(bank(4 + 2 * q + n)[0:CAP, :], hT[:, q, f, :], wd[s][:, f, 512 * n:512 * n + 512],
                                                start=(f == 0), stop=(f == 1))
                    return last

                def silu(q, f):
                    return nc.scalar.activation(sg[:, q, f, :], bank(f)[:, 0:CAP], ACT.Silu)

                def mul_up(q, f):
                    return nc.vector.tensor_tensor(hT[:, q, f, :], sg[:, q, f, :], bank(f)[:, CAP:2 * CAP], ALU.mult)

                @contextmanager
                def further_blocks(eng):
                    count = eng.value_load(over_i[0:1, NOVER:NOVER + 1], min_val=0, max_val=NOVER)
                    with eng.If(count > 0):
                        with eng.Fori(0, count) as m:
                            yield m, count
                        if eng is nc.vector:
                            eng.wait_ge(o_yo, 16 * count + 1)
                            nc.vector.memset(sg[:, 0, 0, 0:1], 0.0).then_inc(s_end, 1)
                            eng.wait_ge(s_end, 1)

                @block.sync
                def _(sp):
                    open_ring(sp, s_xe + s_h + s_ye + s_yo + [o_dn, o_ye, o_yo])
                    for s in range(WSLOTS):
                        load_rows(sp, s, s * CAP, s_in[s])

                    def store(s, i):
                        row = (i * WSLOTS + s) * CAP
                        if not isinstance(row, int):
                            row = sp.snap(row)
                        sp.wait_ge(s_ye[s % 2], 4 * i + 2 * (s // 2) + 3)
                        sp.dma_start(ys_rows[ds(row, CAP), :], ysb[s][:, :]).then_inc(s_yo[s], 16)

                    with sp.Fori(0, ROUNDS - 1) as i:
                        for s in range(WSLOTS):
                            sp.wait_ge(s_dn[s], i + 1)
                            load(sp, s, (i + 1) * WSLOTS + s, ((i + 1) * WSLOTS + s) * CAP, s_in[s])
                            store(s, i)
                    for s in range(WSLOTS):
                        store(s, ROUNDS - 1)
                    for s in range(WSLOTS):
                        sp.wait_ge(s_yo[s], 16 * ROUNDS + 1)
                    with further_blocks(sp) as (m, _):
                        e = sp.value_load(over_i[0:1, ds(m, 1)], min_val=0, max_val=NE - 1)
                        row = sp.snap((m + NE) * CAP)
                        sp.wait_ge(o_dn, m + 1)
                        load(sp, 0, e, row, o_in)
                        sp.wait_ge(o_ye, 2 * m + 3)
                        sp.dma_start(ys_rows[ds(row, CAP), :], ysb[0][:, :]).then_inc(o_yo, 16)

                @block.tensor
                def _(pe):
                    pe.wait_ge(s_in[0], 64)
                    turn_rows(pe, 0, 0, s_xt[0])

                    def body(i, last_round):
                        for s in range(WSLOTS):
                            q, r = s % 2, s // 2
                            pe.wait_ge(s_xe[q], 2 * i + r + 2)
                            gate_up(pe, s, q, 0, s_gu[q])
                            s1, q1 = (s + 1) % WSLOTS, 1 - q
                            more = not (last_round and s == WSLOTS - 1)
                            if more:
                                pe.wait_ge(s_in[s1], 64 * (i + 1 + (s == WSLOTS - 1)))
                            gate_up(pe, s, q, 1, s_gu[q])
                            if more:
                                turn_rows(pe, s1, q1, s_xt[q1])
                            pe.wait_ge(s_ye[q], 4 * i + 2 * r + 1)
                            for f in range(2):
                                pe.wait_ge(s_h[q], 4 * i + 2 * r + f + 2)
                                last = down(pe, s, q, f)
                            last.then_inc(s_dn[s], 1)

                    with pe.Fori(0, ROUNDS - 1) as i:
                        body(i, False)
                    body(ROUNDS - 1, True)
                    with further_blocks(pe) as (m, _):
                        pe.wait_ge(o_in, 64 * m + 64)
                        turn_rows(pe, 0, 0, o_xt, product=True)
                        pe.wait_ge(o_xe, m + 1)
                        for f in range(2):
                            gate_up(pe, 0, 0, f, o_gu)
                        pe.wait_ge(o_h, 2 * m + 2)
                        pe.wait_ge(o_ye, 2 * m + 1)
                        down(pe, 0, 0, 0)
                        down(pe, 0, 0, 1).then_inc(o_dn, 1)

                @block.scalar
                def _(act):
                    def xt_copy(q, value):
                        act.wait_ge(s_xt[q], value)
                        nc.scalar.activation(xsT[q][:, :, :].rearrange("p k c -> p (k c)"), bank(2)[:, 0:KT * CAP], ACT.Copy).then_inc(s_xe[q], 1)

                    xt_copy(0, 1)

                    def body(i, last_round):
                        for s in range(WSLOTS):
                            q, r = s % 2, s // 2
                            for f in range(2):
                                act.wait_ge(s_gu[q], 4 * i + 2 * r + f + 1)
                                act.wait_ge(s_h[q], 4 * i + 2 * r + 1)
                                silu(q, f).then_inc(s_si[q], 1)
                            if not (last_round and s == WSLOTS - 1):
                                q1 = 1 - q
                                xt_copy(q1, 2 * i + (s + 1) // 2 + 1)
                            act.wait_ge(s_dn[s], i + 1)
                            act.wait_ge(s_yo[s], 16 * i + 1)
                            nc.scalar.activation(ysb[s][:, 0:512], bank(4 + 2 * q)[0:CAP, :], ACT.Copy).then_inc(s_ye[q], 1)

                    with act.Fori(0, ROUNDS - 1) as i:
                        body(i, False)
                    body(ROUNDS - 1, True)
                    with further_blocks(act) as (m, _):
                        act.wait_ge(o_xt, m + 1)
                        nc.scalar.activation(xsT[0][:, :, :].rearrange("p k c -> p (k c)"), bank(2)[:, 0:KT * CAP], ACT.Copy).then_inc(o_xe, 1)
                        act.wait_ge(o_gu, 2 * m + 2)
                        silu(0, 0).then_inc(o_si, 1)
                        silu(0, 1).then_inc(o_si, 1)
                        act.wait_ge(o_dn, m + 2)
                        act.wait_ge(o_yo, 16 * m + 1)
                        nc.scalar.activation(ysb[0][:, 0:512], bank(4)[0:CAP, :], ACT.Copy).then_inc(o_ye, 1)

                @block.vector
                def _(dve):
                    def body(i):
                        for s in range(WSLOTS):
                            q, r = s % 2, s // 2
                            for f in range(2):
                                dve.wait_ge(s_si[q], 4 * i + 2 * r + f + 1)
                                dve.wait_ge(s_gu[q], 4 * i + 2 * r + f + 1)
                                mul_up(q, f).then_inc(s_h[q], 1)
                            dve.wait_ge(s_dn[s], i + 1)
                            dve.wait_ge(s_yo[s], 16 * i + 1)
                            nc.vector.tensor_copy(ysb[s][:, 512:D], bank(5 + 2 * q)[0:CAP, :]).then_inc(s_ye[q], 1)

                    with dve.Fori(0, ROUNDS) as i:
                        body(i)
                    with further_blocks(dve) as (m, _):
                        dve.wait_ge(o_si, 2 * m + 2)
                        mul_up(0, 0).then_inc(o_h, 1)
                        mul_up(0, 1).then_inc(o_h, 1)
                        dve.wait_ge(o_dn, m + 2)
                        dve.wait_ge(o_yo, 16 * m + 1)
                        nc.vector.tensor_copy(ysb[0][:, 512:D], bank(5)[0:CAP, :]).then_inc(o_ye, 1)

            with ExitStack() as ph, nc.Block() as block:
                yr = sb("yr" + L, [128, 2 * NT, D], to=ph)
                s_gt, s_cb = [lsem(f"y_back{k}") for k in range(2 * NT)], lsem("y_added")
                junk = sb("junk_c" + L, [128, D], to=ph)

                @block.sync
                def _(sp):
                    if next_norm:
                        next_norm.load(sp)
                    else:
                        for t, rows in TILES:
                            sp.wait_ge(s_cb, 2 * t + 2)
                            dst = y_prompt[0, 128 * t:128 * t + 128, :] if t < 4 else y_sample[:, 0, :]
                            sp.dma_start(dst, x[0:rows, t, :]).then_inc(s_out, 16)
                        sp.wait_ge(s_out, 16 * NT)

                @block.scalar
                def _(act):
                    if next_norm:
                        for t in range(NT):
                            act.wait_ge(s_cb, 2 * t + 2)
                            next_norm.square(act, t, junk)

                @block.gpsimd
                def _(pool):
                    for t, rows in TILES:
                        for k in range(2):
                            pool.indirect_dma_start(out=yr[0:rows, 2 * t + k, :], out_offset=None, in_=ys_rows,
                                                    in_offset=bass.IndirectOffsetOnAxis(ap=pos_i[0:rows, k, t:t + 1], axis=0)
                                                    ).then_inc(s_gt[2 * t + k], 16)
                    if next_norm:
                        pool_do.on(pool)
                        for t in range(NT):
                            next_norm.power(pool, t)
                        pool_do.done()

                @block.vector
                def _(dve):
                    n = 0
                    for t, rows in TILES:
                        for k in range(2):
                            dve.wait_ge(s_gt[2 * t + k], 16)
                            nc.vector.scalar_tensor_tensor(out=x[0:rows, t, :], in0=yr[0:rows, 2 * t + k, :],
                                                           scalar=wts[0:rows, k, t:t + 1], in1=x[0:rows, t, :],
                                                           op0=ALU.mult, op1=ALU.add).then_inc(s_cb, 1)
                            n += 1
                            dve.wait_ge(s_cb, n)

        @scoped
        def layer_b(norm, next_norm):
            phX = ExitStack()
            UW = HD + KQ
            wB = sb("wB", [128, NDIL, KT, UW], to=phB)
            xkT = sb("xkT_b", [128, KT, TOK], to=phX)
            xqT = sb("xqT_b", [128, KT, TOK], to=phX)
            w_kv = a["w_kv_b"].rearrange("(p t) n -> p t n", t=KT)
            w_q = a["w_q_b"][0].rearrange("(p t) n -> p t n", t=KT)

            WINDOW = (1, 2, 0)
            s_w = [sem(f"wb{g}_in") for g in range(NDIL)]

            def kv_cols(j, g, part):
                return ds(g * 512 + part * 256 + j * HD, HD)

            def load_unit(sp, j, g):
                sp.dma_start(wB[:, g, :, 0:HD], w_kv[:, :, kv_cols(j, g, 1)]).then_inc(s_w[g], 16)
                sp.dma_start(wB[:, g, :, HD:2 * HD], w_kv[:, :, kv_cols(j, g, 0)]).then_inc(s_w[g], 16)
                sp.dma_start(wB[:, g, :, 2 * HD:], w_q[:, :, ds(g * D + j * 256, 256)]).then_inc(s_w[g], 16)

            def first_units(sp):
                for g in WINDOW:
                    load_unit(sp, 0, g)

            norm.turn([xkT, xqT], prefetch=first_units)
            w_flat = wB[:, :, :, :].rearrange("p g k n -> p (g k n)")
            out_b = OutProjection("b", a["w_o_b"][0], [w_flat[:, D * m:D * m + D] for m in range(NPAIR)])

            with phX, ExitStack() as ph, nc.Block() as block:
                pT = sb("pT", [128, 3, TOK], to=ph)
                tok = sb("tok", [128, NDIL, NT, UW], to=ph)
                kk = sb("kk", [128, 4, 2 * HD], to=ph)
                kT = sb("kT", [128, SEQ], to=ph)
                qT = sb("qT", [128, 2, SEQ], to=ph)
                vp = sb("vp", [128, 2, 4, HD], to=ph)
                sc = sb("sc", [128, 2, 4, 256], to=ph)
                pTs = sb("pTs", [128, 2, 8 * 128], to=ph)
                nm = sb("nm", [128, 2, 4], to=ph)
                junk = sb("junk_b", [128, 1], to=ph)
                ost = sb("ost", [128, NDIL, 4, 4, HD + 2], to=ph)
                cw = sb("cw", [128, 5, 4, 4], to=ph)
                ce = sb("ce", [128, NDIL, 4, 4], to=ph)
                oc = sb("oc", [128, 4, 4, HD], to=ph)
                ot = gain_row[:, :].rearrange("p (t h e) -> p t h e", t=4, h=4)
                sq = sb("sq", [128, NT, KQ], to=ph)
                rp = sb("rp", [128, 4, NT, 5, 8], to=ph)
                gn = sb("gn", [128, 2, NDIL, HD], to=ph)
                gain = sb("gain", [128, NDIL, KQ], to=ph)
                s_kvo = [sem(f"b_kv_stored{g}") for g in range(NDIL)]
                (s_gn, s_gain, s_proj, s_pev, s_tt, s_tk, s_vc, s_rope, s_tb, s_tbc, s_qk, s_sev, s_mx, s_ex, s_tp,
                 s_ptc, s_pv, s_oc, s_od, s_ob, s_cm, s_ce, s_comb, s_to, s_toc, s_kk) = (
                    sem("b_" + n) for n in (
                        "gains_in", "gain_ready", "proj_done", "proj_copied", "tok_turned", "tok_copied", "v_turn_copied",
                        "rope_done", "qk_turned", "qk_copied", "scores_done", "scores_read", "max_ready",
                        "exp_ready", "p_turned", "p_copied", "pv_done", "o_copied", "o_out", "o_back", "max_diff",
                        "max_exp", "combined", "o_turned", "oT_ready", "k_doubled"))


                def two_on(j, k):
                    return (j, 2) if k == 0 else (j + 1, k - 1)

                @block.sync
                def _(sp):
                    for s in (s_tp, s_pv, s_oc):
                        sp.nop().then_inc(s, 1)
                        sp.nop().then_inc(s, 1)
                    for s in (s_sev, s_ptc):
                        sp.nop().then_inc(s, 1)
                    sp.dma_start(gn[:, 0], a["k_norm_b"].partition_broadcast(128)).then_inc(s_gn, 16)
                    sp.dma_start(gn[:, 1], a["q_norm_b"][0].partition_broadcast(128)).then_inc(s_gn, 16)

                    def next_weights(j, k):
                        sp.wait_ge(s_proj, 6 * (3 * j + k) + 6)
                        load_unit(sp, j + 1, WINDOW[k])

                    def store_kv(j, k):
                        g = WINDOW[k]
                        sp.wait_ge(s_rope, 3 * j + k + 1)
                        out_p, out_s, rows = kv_out[g]
                        t0 = (SEQ - rows) // 128
                        for part, c in ((1, 0), (0, HD)):
                            sp.dma_start(out_p[0, :, part, ds(j, 1), :].rearrange("(t p) a e -> p t (a e)", p=128),
                                         tok[:, g, t0:4, c:c + HD]).then_inc(s_kvo[g], 16)
                            sp.dma_start(out_s[:, 0, part, ds(j, 1), :].rearrange("b a e -> b (a e)"),
                                         tok[0:DEC, g, 4, c:c + HD]).then_inc(s_kvo[g], 16)
                        sp.dma_start(q_rows[g, :, ds(j, 1), :].rearrange("b a e -> b (a e)"), tok[0:DEC, g, 4, 2 * HD:]).then_inc(s_kvo[g], 16)

                    def reorder(j, k):
                        g = WINDOW[k]
                        sp.wait_ge(s_oc, 4 * (3 * j + k) + 4 + 2)
                        sp.dma_start(o_rows[g - 1].rearrange("(i r) x -> i (r x)", r=4),
                                     ost[:, g].rearrange("p r h e -> p (r h e)")).then_inc(s_od, 16)
                        sp.wait_ge(s_od, 16 * (2 * j + g))
                        sp.dma_start(ost[:, g].rearrange("p t h e -> p t (h e)"),
                                     o_rows[g - 1].rearrange("(t p) x -> p t x", p=128)).then_inc(s_ob, 16)

                    for k in range(2):
                        next_weights(0, k)
                    store_kv(0, 0)

                    def body(j, left):
                        for k in range(NDIL):
                            if left == 0 and k == 1:
                                sp.wait_ge(s_proj, 6 * NDIL * NKV)
                                out_b.load(sp, range(NPAIR))
                            if left >= (1 if k == 0 else 2):
                                next_weights(*two_on(j, k))
                            if left or k < 2:
                                store_kv(*((j, k + 1) if k < 2 else (j + 1, 0)))
                            if k < 2:
                                reorder(j, k)

                    with sp.Fori(0, NKV - 2) as j:
                        body(j, 2)
                    body(NKV - 2, 1)
                    body(NKV - 1, 0)
                    for g in range(NDIL):
                        sp.wait_ge(s_kvo[g], 80 * NKV)

                @block.tensor
                def _(pe):
                    def project(j, k, f, h):
                        n, g = 3 * j + k, WINDOW[k]
                        if f == 0:
                            if h == 0:
                                pe.wait_ge(s_w[g], 48 * j + 48)
                            if not (isinstance(n, int) and n == 0):
                                if h == 0:
                                    pe.wait_ge(s_tk, 5 * n)
                                else:
                                    pe.wait_ge(s_vc, n)
                        else:
                            pe.wait_ge(s_pev, 6 * n + 2 * (f - 1) + h + 1)
                        xT = xkT if f == 0 else xqT
                        for kt in range(KT):
                            last = nc.tensor.matmul(bank(h)[:, 0:HALF], wB[:, g, kt, 128 * f:128 * f + 128],
                                                    xT[:, kt, HALF * h:HALF * h + HALF], start=(kt == 0), stop=(kt == KT - 1))
                        last.then_inc(s_proj, 1)

                    def turn_tok(j, k, t):
                        n, rows = 3 * j + k, TILES[t][1]
                        if t < 2:
                            pe.wait_ge(s_pev, 6 * n + 6)
                        else:
                            pe.wait_ge(s_tk, 5 * n + (t - 1 if t < 4 else 4))
                        for f in range(3):
                            last = nc.tensor.transpose(bank(t % 2)[0:rows, 128 * f:128 * f + 128],
                                                       pT[:, f, 128 * t:128 * t + rows], ident)
                        last.then_inc(s_tt, 1)
                        if t == 4 and WINDOW[k]:
                            for r in range(4):
                                last = nc.tensor.transpose(bank(1)[:, HD * r:HD * r + HD], pT[0:HD, 0, r:SEQ:4], ident[0:HD, 0:HD])
                            last.then_inc(s_tt, 1)

                    def front(j, k):
                        for f in range(3):
                            for h in range(2):
                                project(j, k, f, h)
                        for t in range(NT):
                            turn_tok(j, k, t)

                    def weave(j, k, more, turned):
                        n, g = 3 * j + k, WINDOW[k]

                        def ahead(step, *at):
                            if more:
                                step(*two_on(j, k), *at)

                        def turn_back(f):
                            for t in range(4):
                                src = kk[:, t, :] if f == 2 else tok[:, g, t, 128 * f + 128:128 * f + 256]
                                last = nc.tensor.transpose(bank(6 + f % 2)[:, 128 * t:128 * t + 128], src, ident)
                            last.then_inc(s_tb, 1)

                        def qk(h):
                            rows = slice(64 * (h % 2), 64 * (h % 2) + 64)
                            pe.wait_ge(s_sev, 4 * n + h + 1)
                            q, k = qT[rows, h // 2, :], kT[rows, :]
                            for b in range(4):
                                if g == 0:
                                    o = ps[:, 2048 + 256 * b:2048 + 256 * b + 256]
                                    if b:
                                        last = nc.tensor.matmul(o, q[:, 128 * b:128 * b + 128], k[:, 128 * b - 128:128 * b + 128],
                                                                start=True, stop=True)
                                    else:
                                        for half in range(2):
                                            nc.tensor.matmul(o[:, 128 * half:128 * half + 128], q[:, 0:128], k[:, 0:128],
                                                             start=True, stop=True)
                                else:
                                    last = nc.tensor.matmul(bank(4)[:, 128 * b:128 * b + 128], q[:, b:SEQ:4], k[:, b:SEQ:4],
                                                            start=True, stop=True)
                            last.then_inc(s_qk, 1)

                        def turn_p(h):
                            pe.wait_ge(s_ex, 4 * n + h + 1)
                            pe.wait_ge(s_ptc, 4 * n + h + 1)
                            for b in range(4):
                                for half in range(2 if g == 0 else 1):
                                    o = 3072 + (256 * b + 128 * half if g == 0 else 128 * b)
                                    last = nc.tensor.transpose(ps[:, o:o + 128], sc[:, h % 2, b, 128 * half:128 * half + 128], ident)
                            last.then_inc(s_tp, 1)

                        def pv(h):
                            pe.wait_ge(s_ptc, 4 * n + h + 2)
                            pe.wait_ge(s_oc, 4 * n + h + 1)
                            for b in range(4):
                                o = bank(2 + h % 2)[:, HD * b:HD * b + HD]
                                if g == 0:
                                    for half in ((0, 1) if b else (1,)):
                                        c = 256 * b + 128 * half
                                        last = nc.tensor.matmul(o, pTs[:, h % 2, c:c + 128], tok[:, 0, b - 1 + half, 0:HD],
                                                                start=(half == 0 or b == 0), stop=(half == 1))
                                else:
                                    last = nc.tensor.matmul(o, pTs[:, h % 2, 128 * b:128 * b + 128], vp[:, g - 1, b, :],
                                                            start=True, stop=True)
                            last.then_inc(s_pv, 1)

                        pe.wait_ge(s_rope, n + 1)
                        pe.wait_ge(s_ptc, 4 * n + 1)
                        turn_back(0)
                        turn_back(1)
                        ahead(project, 0, 0)
                        pe.wait_ge(s_tbc, 3 * n + 1)
                        pe.wait_ge(s_kk, n + 1)
                        turn_back(2)
                        ahead(project, 0, 1)
                        pe.wait_ge(s_tbc, 3 * n + 3)
                        qk(0)
                        ahead(project, 1, 0)
                        if turned:
                            turn_o(j - 1)
                        qk(1)
                        if turned:
                            pe.wait_ge(s_toc, j)
                        turn_p(0)
                        ahead(project, 1, 1)
                        qk(2)
                        turn_p(1)
                        pv(0)
                        ahead(project, 2, 0)
                        qk(3)
                        turn_p(2)
                        pv(1)
                        ahead(project, 2, 1)
                        ahead(turn_tok, 0)
                        ahead(turn_tok, 1)
                        turn_p(3)
                        pv(2)
                        ahead(turn_tok, 2)
                        ahead(turn_tok, 3)
                        pv(3)
                        ahead(turn_tok, 4)

                    def turn_o(j):
                        pe.wait_ge(s_comb, j + 1)
                        for f in range(2):
                            for t in range(4):
                                last = nc.tensor.transpose(bank(6 + f)[:, 128 * t:128 * t + 128], flat(oc[:, t, 2 * f:2 * f + 2, :]), ident)
                        last.then_inc(s_to, 1)

                    front(0, 0)
                    front(0, 1)

                    def body(j, first, last):
                        for k in range(NDIL):
                            weave(j, k, not last or k == 0, k == 0 and not first)

                    body(0, True, False)
                    with pe.Fori(1, NKV - 1) as j:
                        body(j, False, False)
                    body(NKV - 1, False, True)
                    turn_o(NKV - 1)

                @block.scalar
                def _(act):
                    def proj_copy(j, k, f, h):
                        act.wait_ge(s_proj, 6 * (3 * j + k) + 2 * f + h + 1)
                        nc.scalar.activation(pT[:, f, HALF * h:HALF * h + HALF], bank(h)[:, 0:HALF], ACT.Copy).then_inc(s_pev, 1)

                    def front(j, k):
                        for f in range(3):
                            for h in range(2):
                                proj_copy(j, k, f, h)

                    def weave(j, k, more):
                        n, g = 3 * j + k, WINDOW[k]

                        def ahead(*at):
                            if more:
                                proj_copy(*two_on(j, k), *at)

                        def turned_copy(f):
                            act.wait_ge(s_tb, 3 * n + f + 1)
                            dst = kT[:, :] if f == 2 else qT[:, f, :]
                            nc.scalar.activation(dst, bank(6 + f % 2), ACT.Copy).then_inc(s_tbc, 1)

                        def exps(h):
                            act.wait_ge(s_mx, 4 * n + h + 1)
                            width = 256 if g == 0 else 128
                            for b in range(4):
                                last = nc.scalar.activation(sc[:, h % 2, b, 0:width], sc[:, h % 2, b, 0:width], ACT.Exp,
                                                            bias=nm[:, h % 2, b:b + 1], accum_out=ost[:, g, b, h, HD + 1:HD + 2])
                            last.then_inc(s_ex, 1)

                        def p_copy(h):
                            act.wait_ge(s_tp, 4 * n + h + 1 + 2)
                            act.wait_ge(s_pv, 4 * n + h + 1)
                            width = 1024 if g == 0 else 512
                            nc.scalar.activation(pTs[:, h % 2, 0:width], ps[:, 3072:3072 + width], ACT.Copy).then_inc(s_ptc, 1)

                        act.wait_ge(s_rope, n + 1)
                        nc.scalar.activation(kk[:, :, :].rearrange("p t (a e) -> p t a e", a=2),
                                             tok[:, g, 0:4, HD:2 * HD].unsqueeze(2).to_broadcast([128, 4, 2, HD]),
                                             ACT.Copy).then_inc(s_kk, 1)
                        turned_copy(0)
                        turned_copy(1)
                        ahead(0, 0)
                        turned_copy(2)
                        ahead(0, 1)
                        exps(0)
                        ahead(1, 0)
                        p_copy(0)
                        exps(1)
                        ahead(1, 1)
                        p_copy(1)
                        exps(2)
                        ahead(2, 0)
                        p_copy(2)
                        exps(3)
                        ahead(2, 1)
                        p_copy(3)

                    front(0, 0)
                    front(0, 1)

                    def body(j, last):
                        for k in range(NDIL):
                            weave(j, k, not last or k == 0)
                        act.wait_ge(s_cm, j + 1)
                        nc.scalar.activation(ce[:, :, :, :], ce[:, :, :, :], ACT.Exp).then_inc(s_ce, 1)

                    with act.Fori(0, NKV - 1) as j:
                        body(j, False)
                    body(NKV - 1, True)

                @block.vector
                def _(dve):
                    dve_do.on(dve)
                    V = nc.vector
                    dve_do(V.memset(tok[:, :, 4, :], 0.0))
                    dve.wait_ge(s_gn, 32)
                    dve_do(V.tensor_scalar(gain[:, :, 0:HD], gn[:, 0], HD ** 0.5, None, ALU.mult))
                    V.tensor_scalar(gain[:, :, HD:].rearrange("p g (h e) -> p g h e", h=4),
                                    gn[:, 1].unsqueeze(2).to_broadcast([128, NDIL, 4, HD]), HD ** 0.5, None, ALU.mult).then_inc(s_gain, 1)
                    dve_do.done()

                    def tok_copy(j, k, t):
                        n, g, rows = 3 * j + k, WINDOW[k], TILES[t][1]
                        if t == 0 and (not isinstance(j, int) or j):
                            dve.wait_ge(s_kvo[g], 80 * j)
                            dve.wait_ge(s_tb, 3 * (n - 2))
                            if g == 0:
                                dve.wait_ge(s_pv, 4 * (n - 2) + 2)
                        tt = 5 * n + 2 * j + k
                        dve.wait_ge(s_tt, tt + t + 1)
                        V.tensor_copy(tok[0:rows, g, t, :], bank(t % 2)[0:rows, 0:UW]).then_inc(s_tk, 1)
                        if t == 4:
                            if g:
                                dve.wait_ge(s_tt, tt + 6)
                                V.tensor_copy(flat(vp[:, g - 1]), bank(1)[:, 0:4 * HD]).then_inc(s_vc, 1)
                            else:
                                V.memset(junk[:, :], 0.0).then_inc(s_vc, 1)

                    def weave(j, k, more, turned):
                        n, g = 3 * j + k, WINDOW[k]

                        def ahead(t):
                            if more:
                                tok_copy(*two_on(j, k), t)

                        def soft(h):
                            dve.wait_ge(s_qk, 4 * n + h + 1)
                            dve.wait_ge(s_tp, 4 * n + h + 1)
                            if g == 0:
                                dst, src = sc[:, h % 2, :, :], ps[:, 2048:3072].rearrange("p (b k) -> p b k", b=4)
                                mask = C("m0").rearrange("p (b k) -> p b k", b=4)
                            else:
                                dst, src = sc[:, h % 2, :, 0:128], bank(4).rearrange("p (b k) -> p b k", b=4)
                                mask = C(f"m{g}").unsqueeze(1).to_broadcast([128, 4, 128])
                            V.scalar_tensor_tensor(out=dst, in0=src, scalar=SCALE, in1=mask, op0=ALU.mult, op1=ALU.add).then_inc(s_sev, 1)
                            dve.wait_ge(s_sev, 4 * n + h + 2)
                            top = ost[:, g, :, h, HD:HD + 1].rearrange("p b a -> p (b a)")
                            dve_do(V.tensor_reduce(top, dst, AX_X, ALU.max))
                            V.tensor_scalar(nm[:, h % 2, :], top, -1.0, None, ALU.mult).then_inc(s_mx, 1)

                        def o_copy(h):
                            dve.wait_ge(s_pv, 4 * n + h + 1 + 2)
                            V.tensor_copy(ost[:, g, :, h, 0:HD], bank(2 + h % 2)[:, 0:4 * HD].rearrange("p (b e) -> p b e", b=4)).then_inc(s_oc, 1)

                        soft(0)
                        if turned:
                            turn_copy(j - 1)
                        soft(1)
                        soft(2)
                        o_copy(0)
                        soft(3)
                        o_copy(1)
                        ahead(0)
                        ahead(1)
                        o_copy(2)
                        ahead(2)
                        ahead(3)
                        o_copy(3)
                        ahead(4)

                    def combine(j):
                        dve.wait_ge(s_ob, 32 * j + 32)

                        def mx(g):
                            return ost[:, g, :, :, HD:HD + 1].rearrange("p t h a -> p t (h a)")

                        def sm(g):
                            return ost[:, g, :, :, HD + 1:HD + 2].rearrange("p t h a -> p t (h a)")

                        dve.wait_ge(s_oc, 12 * j + 14)
                        dve_do(V.tensor_tensor(cw[:, 0], mx(0), mx(1), ALU.max))
                        dve_do(V.tensor_tensor(cw[:, 0], cw[:, 0], mx(2), ALU.max))
                        for g in range(NDIL):
                            ins = V.tensor_tensor(ce[:, g], mx(g), cw[:, 0], ALU.subtract)
                            if g < 2:
                                dve_do(ins)
                        ins.then_inc(s_cm, 1)
                        dve.wait_ge(s_ce, j + 1)
                        for g in range(NDIL):
                            dve_do(V.tensor_tensor(cw[:, 1 + g], ce[:, g], sm(g), ALU.mult))
                        dve_do(V.tensor_tensor(cw[:, 1], cw[:, 1], cw[:, 2], ALU.add))
                        dve_do(V.tensor_tensor(cw[:, 1], cw[:, 1], cw[:, 3], ALU.add))
                        dve_do(V.reciprocal(cw[:, 4], cw[:, 1]))
                        for g in range(NDIL):
                            dve_do(V.tensor_tensor(ce[:, g], ce[:, g], cw[:, 4], ALU.mult))
                        for g in range(NDIL):
                            dve_do(V.tensor_tensor((ot if g else oc)[:, :, :, :], ost[:, g, :, :, 0:HD],
                                                   ce[:, g].unsqueeze(3).to_broadcast([128, 4, 4, HD]), ALU.mult))
                            if g:
                                ins = V.tensor_tensor(oc[:, :, :, :], oc[:, :, :, :], ot[:, :, :, :], ALU.add)
                                if g < 2:
                                    dve_do(ins)
                        ins.then_inc(s_comb, 1)

                    def turn_copy(j):
                        dve.wait_ge(s_to, j + 1)
                        V.tensor_copy(oT[:, ds(2 * j, 2), 0:SEQ], bank(6, 2).rearrange("p (f m) -> p f m", f=2)).then_inc(s_toc, 1)

                    for k in range(2):
                        for t in range(NT):
                            tok_copy(0, k, t)

                    def body(j, first, last):
                        for k in range(NDIL):
                            weave(j, k, not last or k == 0, k == 0 and not first)
                        combine(j)

                    per = 3 * 4 + 2 + 2 + 3 + 2 + 1 + 3 + 3 + 1
                    dve_do.enter(0, per)
                    body(0, True, False)
                    dve_do.leave(1)
                    with dve.Fori(1, NKV - 1) as j:
                        dve_do.enter(j - 1, per)
                        body(j, False, False)
                    dve_do.leave(NKV - 2)
                    dve_do.enter(0, per)
                    body(NKV - 1, False, True)
                    dve_do.leave(1)
                    turn_copy(NKV - 1)

                @block.gpsimd
                def _(pool):
                    pool_do.on(pool)
                    P = nc.gpsimd
                    pool.wait_ge(s_gain, 1)

                    def front(j, k):
                        n, g = 3 * j + k, WINDOW[k]
                        pool.wait_ge(s_tk, 5 * n + 5)
                        kq = tok[:, g, :, HD:]
                        s4 = sq[:, :, :].rearrange("p t (h e) -> p t h e", h=5)
                        pool_do(P.tensor_tensor(sq[:, :, :], kq, kq, ALU.mult))
                        w = HD // 2
                        while w:
                            pool_do(P.tensor_tensor(s4[:, :, :, 0:w], s4[:, :, :, 0:w], s4[:, :, :, w:2 * w], ALU.add))
                            w //= 2
                        ss = s4[:, :, :, 0]
                        shape = [128, NT, 5]
                        pool_do(P.tensor_tensor(ss, ss, C("eps64").unsqueeze(2).to_broadcast(shape), ALU.add))
                        pool_do(P.tensor_tensor(ss, ss, C("mhalf").unsqueeze(2).to_broadcast(shape), ALU.pow))
                        k4 = kq.rearrange("p t (h e) -> p t h e", h=5)
                        pool_do(P.tensor_tensor(k4, k4, s4[:, :, :, 0:1].to_broadcast([128, NT, 5, HD]), ALU.mult))
                        pool_do(P.tensor_tensor(kq, kq, gain[:, g, :].unsqueeze(1).to_broadcast([128, NT, KQ]), ALU.mult))
                        x1, x2 = k4[:, :, :, 0:8], k4[:, :, :, 8:16]
                        cos, sin = (C(m).rearrange("p (t e) -> p t e", e=8).unsqueeze(2).to_broadcast([128, NT, 5, 8])
                                    for m in ("cos", "sin"))
                        pool_do(P.tensor_tensor(rp[:, 0], x1, cos, ALU.mult))
                        pool_do(P.tensor_tensor(rp[:, 1], x2, sin, ALU.mult))
                        pool_do(P.tensor_tensor(rp[:, 2], x2, cos, ALU.mult))
                        pool_do(P.tensor_tensor(rp[:, 3], x1, sin, ALU.mult))
                        pool_do(P.tensor_tensor(x1, rp[:, 0], rp[:, 1], ALU.subtract))
                        P.tensor_tensor(x2, rp[:, 2], rp[:, 3], ALU.add).then_inc(s_rope, 1)

                    per = 3 * 16
                    with pool.Fori(0, NKV) as j:
                        pool_do.enter(j, per)
                        for k in range(NDIL):
                            front(j, k)
                    pool_do.leave(NKV)

            n1, n2 = PAST // 4 + 1, PAST // 16 + 1
            with ExitStack() as ph, nc.Block() as block:
                kb = sb("kb", [128, DEC, 2, 512], to=ph)
                qb = sb("qb", [128, 2, DEC, D], to=ph)
                oh_b = sb("oh_b", [128, 2, NKV * HD], to=ph)
                s_oh0, s_ohc, s_ot = (sem("bs_" + n) for n in ("heads_zeroed", "heads_copied", "heads_turned"))
                prod = sb("prodb", [128, D], to=ph)
                junk = sb("junk_s", [128, D], to=ph)
                SS = sb("SS", [128, 2, DEC, NH], to=ph)
                pr = sb("pr", [128, 256], to=ph)
                pt = sb("ptb", [128, 2, 128], to=ph)
                sml = sb("sml", [128, 4], to=ph)
                s_kb = [[sem(f"bs_keys_in{b}_{tile}") for tile in range(2)] for b in range(DEC)]
                s_own = sem("bs_own_in")
                s_e, s_z, s_st, s_mm, s_xx, s_pn, s_pt, s_pc, s_pv, s_fin = (
                    sem("bs_" + n) for n in ("prod_done", "scores", "turned", "max", "exp", "normed",
                                             "p_turned", "p_copied", "pv_done", "o_ready"))
                ranges = ((1, 0, n1), (2, n1, n1 + n2), (0, n1 + n2, S1ROWS))

                @block.sync
                def _(sp):
                    next_norm.load(sp)

                    def queries(g, b, rows, tile, lo):
                        q = q_rows[g, b].partition_broadcast(rows)
                        sp.dma_start(qb[lo:lo + rows, tile, b, :].rearrange("p (j e) -> p j e", j=NKV), q).then_inc(s_kb[b][tile], 16)

                    for b in range(DEC):
                        queries(0, b, 128, 0, 0)
                        sp.dma_start(kb[:, b, 0, :], a["cache_kv_b1"][b].rearrange("s c h e -> s (c h e)")).then_inc(s_kb[b][0], 16)
                        if b == 0:
                            for g, lo, hi in ranges:
                                sp.dma_start(kb[hi - 1:hi, :, 1, :], kv_out[g][1].rearrange("b a c h e -> a b (c h e)")).then_inc(s_own, 16)
                        for g, lo, hi in ranges:
                            queries(g, b, hi - lo, 1, lo)
                        sp.dma_start(kb[0:n1 - 1, b, 1, :], a["cache_kv_b2"][b, 0:PAST:4].rearrange("s c h e -> s (c h e)")).then_inc(s_kb[b][1], 16)
                        sp.dma_start(kb[n1:n1 + n2 - 1, b, 1, :], a["cache_kv_b3"][b, 0:PAST:16].rearrange("s c h e -> s (c h e)")).then_inc(s_kb[b][1], 16)

                @block.tensor
                def _(pe):
                    for i in range(8):
                        out_b.product(pe, i)
                    pe.wait_ge(s_z, 2 * DEC + 1)
                    for tile in range(2):
                        last = nc.tensor.transpose(bank(4)[:, 128 * tile:128 * tile + 128], SS[:, tile].rearrange("p b h -> p (b h)"), ident)
                    last.then_inc(s_st, 1)
                    pe.wait_ge(s_pn, 1)
                    for tile in range(2):
                        last = nc.tensor.transpose(bank(5)[:, 128 * tile:128 * tile + 128], pr[:, 128 * tile:128 * tile + 128], ident)
                    last.then_inc(s_pt, 1)
                    pe.wait_ge(s_pc, 1)
                    for b in range(DEC):
                        for tile, rows in ((0, 128), (1, S1ROWS)):
                            last = nc.tensor.matmul(bank(b // 4)[32 * (b % 4):32 * (b % 4) + NH, 0:NKV * HD],
                                                    pt[0:rows, tile, NH * b:NH * b + NH], kb[0:rows, b, tile, 256:512],
                                                    start=(tile == 0), stop=(tile == 1))
                        if b % 4 == 3:
                            last.then_inc(s_pv, 1)
                    own = ident.rearrange("p (i h) -> p i h", i=4)
                    for q in range(2):
                        pe.wait_ge(s_ohc, 4 * q + 4)
                        for j in range(NKV):
                            for i in range(2):
                                o = 32 * q + 8 * j
                                last = nc.tensor.matmul(bank(4)[64 * i:64 * i + 64, o:o + 8], oh_b[:, q, HD * j:HD * j + HD],
                                                        own[:, :, 4 * j + i:4 * j + i + 3:2], start=True, stop=True)
                    last.then_inc(s_ot, 1)
                    pe.wait_ge(s_fin, 2)
                    for i in (8, 9):
                        out_b.product(pe, i)

                @block.vector
                def _(dve):
                    dve_do.on(dve)
                    V = nc.vector
                    V.memset(flat(oh_b), 0.0).then_inc(s_oh0, 1)
                    V.memset(SS[:, 1, :, :], NEG).then_inc(s_z, 1)
                    dve.wait_ge(s_z, 1)
                    for u in range(2 * DEC):
                        b, tile = u // 2, u % 2
                        rows = 128 if tile == 0 else S1ROWS
                        dve.wait_ge(s_kb[b][tile], 16 * (5 if tile else 2))
                        if u == 1:
                            dve.wait_ge(s_own, 16 * NDIL)
                        shape = [rows, NKV, 4, HD]
                        V.tensor_tensor(prod[0:rows, :].rearrange("p (j i e) -> p j i e", j=NKV, i=4),
                                        kb[0:rows, b, tile, 0:256].rearrange("p (j e) -> p j e", j=NKV).unsqueeze(2).to_broadcast(shape),
                                        qb[0:rows, tile, b, :].rearrange("p (j i e) -> p j i e", j=NKV, i=4), ALU.mult).then_inc(s_e, 1)
                        dve.wait_ge(s_e, u + 1)
                        V.reduce_sum(SS[0:rows, tile, b, :], prod[0:rows, :].rearrange("p (h e) -> p h e", e=HD), AX_X).then_inc(s_z, 1)
                        dve.wait_ge(s_z, u + 2)
                        if tile and b:
                            out_b.add(dve, b - 1)
                    out_b.add(dve, DEC - 1)
                    dve.wait_ge(s_st, 1)
                    dve_do(V.tensor_scalar(pr[:, :], bank(4)[:, 0:256], SCALE, None, ALU.mult))
                    dve_do(V.tensor_reduce(sml[:, 0:1], pr[:, :], AX_X, ALU.max))
                    V.tensor_scalar(sml[:, 1:2], sml[:, 0:1], -1.0, None, ALU.mult).then_inc(s_mm, 1)
                    dve.wait_ge(s_xx, 1)
                    dve_do(V.reciprocal(sml[:, 3:4], sml[:, 2:3]))
                    V.tensor_scalar(pr[:, :], pr[:, :], sml[:, 3:4], None, ALU.mult).then_inc(s_pn, 1)
                    dve.wait_ge(s_pt, 1)
                    V.tensor_copy(pt[:, :, :].rearrange("p a b -> p (a b)"), bank(5)[:, 0:256]).then_inc(s_pc, 1)
                    dve.wait_ge(s_oh0, 1)
                    for q in range(2):
                        dve.wait_ge(s_pv, q + 1)
                        for i in range(4):
                            rows = slice(32 * i, 32 * i + NH)
                            V.tensor_copy(oh_b[rows, q, :], bank(q)[rows, 0:NKV * HD]).then_inc(s_ohc, 1)
                    dve.wait_ge(s_ot, 1)
                    for q in range(2):
                        V.tensor_copy(oT[:, :, SEQ + 4 * q:SEQ + 4 * q + 4].rearrange("p (j m) i -> p j m i", m=2),
                                      bank(4)[:, 32 * q:32 * q + 32].rearrange("p (j i m) -> p j m i", j=NKV, i=4)).then_inc(s_fin, 1)
                    for i in (8, 9):
                        out_b.add(dve, i)
                    dve_do.done()

                @block.scalar
                def _(act):
                    def square(t):
                        act.wait_ge(out_b.s_added, 2 * t + 2)
                        next_norm.square(act, t, junk)

                    for t in range(3):
                        square(t)
                    act.wait_ge(s_mm, 1)
                    nc.scalar.activation(pr[:, :], pr[:, :], ACT.Exp, bias=sml[:, 1:2], accum_out=sml[:, 2:3]).then_inc(s_xx, 1)
                    square(3)
                    square(4)

                @block.gpsimd
                def _(pool):
                    pool_do.on(pool)
                    for t in range(NT):
                        next_norm.power(pool, t)
                    pool_do.done()

        s_out = sem("y_stored")
        norm_b, norm_ffn1 = Norm([a["g_kv"], a["g_attn"][1]]), Norm([a["g_ffn"][1]])
        with ExitStack() as phM:
            moe(0, norm, norm_b)
        with ExitStack() as phB:
            layer_b(norm_b, norm_ffn1)
        with ExitStack() as phM:
            moe(1, norm_ffn1, None)


_INS = ["x_prompt", "x_sample", "cache_kv_a", "cache_kv_b1", "cache_kv_b2", "cache_kv_b3", "page_table", "g_attn", "g_ffn",
        "w_qkv_a", "w_o_a", "sb_bias", "g_kv", "w_kv_b", "k_norm_b", "w_q_b", "q_norm_b", "w_o_b", "w_router_group",
        "b_router_group", "w_router_expert", "b_router_expert", "w_gate", "w_up", "w_down"]
_OUTS = [(1, SEQ, D), (DEC, 1, D), (1, 1, SEQ, 2, NH, HD), (1, DEC, 1, 2, NH, HD),
         (1, 128, 2, NKV, HD), (DEC, 1, 2, NKV, HD), (1, SEQ, 2, NKV, HD), (DEC, 1, 2, NKV, HD),
         (1, SEQ, 2, NKV, HD), (DEC, 1, 2, NKV, HD)]


def kernel(**inputs):
    import numpy as _np
    import concourse.bacc as _bacc
    from concourse import mybir as _mybir
    from concourse.bass_utils import run_bass_kernel_spmd as _run

    nc = _bacc.Bacc("TRN2", target_bir_lowering=False, num_devices=1)
    arrays, aps = {}, {}
    given = {name: _np.ascontiguousarray(inputs[name]) for name in _INS}
    given["const"] = constants()
    for name, arr in given.items():
        arrays[f"in_{name}"] = arr
        aps[name] = nc.dram_tensor(f"in_{name}", arr.shape, _mybir.dt.from_np(arr.dtype), kind="ExternalInput").ap()
    outs = [nc.dram_tensor(f"out_{i}", shape, _mybir.dt.float32, kind="ExternalOutput").ap() for i, shape in enumerate(_OUTS)]
    build(nc, aps, outs)
    r = _run(nc, [arrays], core_ids=[0])
    return tuple(r.results[0][f"out_{i}"] for i in range(len(_OUTS)))
```
